# Optimizing a Trainium2 kernel written in Bass

```python
import math
import jax, jax.numpy as jnp
from jax import lax
import numpy as np

D_MODEL = 1024
BATCH = 1
SEQ = 128
DEPTH = 2
DEC_BATCH = 1
DEC_SEQ = 512
PAST_LEN = 128

GRID_W = 64
N_EVEN = (DEPTH + 1) // 2
N_ODD = DEPTH // 2
NORM_EPS = 1e-6
NEG_BIG = -1e30
HEAD_DIM = 64
N_Q_HEADS = D_MODEL // 128
N_KV_HEADS = N_Q_HEADS // 4
GQA_GROUP = N_Q_HEADS // N_KV_HEADS
WINDOW = 128
ATTN_BLOCK = 128
ROPE_THETA = 10000.0
SSD_HEADS = D_MODEL // 128
SSD_HEAD_DIM = 64
SSD_D_INNER = SSD_HEADS * SSD_HEAD_DIM
SSD_GROUPS = 2
D_STATE = 64
CONV_K = 5
SSD_CHUNK = 64
SSD_CONV_DIM = SSD_D_INNER + 2 * SSD_GROUPS * D_STATE
ATTN_Q_DIM = N_Q_HEADS * HEAD_DIM
ATTN_KV_DIM = N_KV_HEADS * HEAD_DIM
EVEN_SPLITS = (ATTN_Q_DIM,
               ATTN_Q_DIM + ATTN_KV_DIM,
               ATTN_Q_DIM + 2 * ATTN_KV_DIM,
               ATTN_Q_DIM + 2 * ATTN_KV_DIM + SSD_D_INNER,
               ATTN_Q_DIM + 2 * ATTN_KV_DIM + SSD_D_INNER + SSD_CONV_DIM)
EVEN_IN = EVEN_SPLITS[-1] + 2 * SSD_HEADS
EVEN_MIX = ATTN_Q_DIM + SSD_D_INNER
HGRN_HEADS = D_MODEL // 128
HGRN_DK = 128
HGRN_DV = D_MODEL // HGRN_HEADS
HGRN_KW = HGRN_HEADS * HGRN_DK
HGRN_VW = HGRN_HEADS * HGRN_DV
HGRN_SPLITS = (HGRN_KW, 2 * HGRN_KW, 3 * HGRN_KW, 3 * HGRN_KW + HGRN_VW)
HGRN_IN = 3 * HGRN_KW + 2 * HGRN_VW
HGRN_CHUNK = 32
PEER_HEADS = 8
PEER_NKEYS = 128
PEER_EXPERTS = PEER_NKEYS * PEER_NKEYS
PEER_TOPK = 16
PEER_DKEY = 128
PEER_BLOCK = 128

kernel_name = 'hybrid_diffusion_swa_ssd_hgrn2_peer_step'

F32 = jnp.float32

def rms_norm(x, w):
    xf = x.astype(F32)
    y = xf * lax.rsqrt(jnp.mean(xf * xf, axis=-1, keepdims=True) + NORM_EPS)
    return (y * w.astype(F32)).astype(x.dtype)

def modulation(cond, w_ada, b_ada):
    m = jax.nn.silu(cond) @ w_ada + b_ada
    return jnp.split(m[:, None, :], 6, axis=-1)

def depthwise_conv(x, w, b):
    c = x.shape[-1]
    pad = (CONV_K - 1) // 2
    y = lax.conv_general_dilated(x, w[:, None, :].astype(x.dtype), window_strides=(1,),
                                 padding=((pad, pad),), dimension_numbers=('NWC', 'WIO', 'NWC'),
                                 feature_group_count=c)
    return y + b.astype(x.dtype)

def axial_rope(x):
    t = x.shape[1]
    n_rows = t // GRID_W
    rows = jnp.repeat(jnp.arange(n_rows, dtype=F32), GRID_W)
    cols = jnp.tile(jnp.arange(GRID_W, dtype=F32), n_rows)
    axis_dim = HEAD_DIM // 2
    inv_freq = ROPE_THETA ** (-jnp.arange(0, axis_dim, 2, dtype=F32) / axis_dim)

    def rotate(xa, pos):
        ang = pos[:, None] * inv_freq[None, :]
        cos = jnp.cos(ang)[None, :, None, :]
        sin = jnp.sin(ang)[None, :, None, :]
        x1, x2 = jnp.split(xa.astype(F32), 2, axis=-1)
        return jnp.concatenate([x1 * cos - x2 * sin, x2 * cos + x1 * sin], axis=-1)

    out = jnp.concatenate([rotate(x[..., :axis_dim], rows), rotate(x[..., axis_dim:], cols)], axis=-1)
    return out.astype(x.dtype)

def chunked_gated_scan(q, k, v, log_g, s0, chunk):
    b, t, h, _ = q.shape
    n = t // chunk
    out_dtype = v.dtype

    def to_chunks(a):
        return a.astype(F32).reshape(b, n, chunk, h, a.shape[-1]).transpose(1, 0, 3, 2, 4)

    qc, kc, vc, gc = (to_chunks(a) for a in (q, k, v, log_g))
    causal = jnp.tril(jnp.ones((chunk, chunk), dtype=bool))
    scalar = log_g.shape[-1] == 1

    def step(s, xs):
        qi, ki, vi, gi = xs
        cum = jnp.cumsum(gi, axis=2)
        last = cum[:, :, -1:, :]
        if scalar:
            seg = cum[..., 0][:, :, :, None] - cum[..., 0][:, :, None, :]
            decay = jnp.exp(jnp.where(causal, seg, NEG_BIG))
            scores = jnp.einsum('bhtk,bhsk->bhts', qi, ki) * decay
        else:
            seg = cum[:, :, :, None, :] - cum[:, :, None, :, :]
            decay = jnp.exp(jnp.where(causal[..., None], seg, NEG_BIG))
            scores = jnp.einsum('bhtk,bhsk,bhtsk->bhts', qi, ki, decay)
        o = (jnp.einsum('bhts,bhsv->bhtv', scores, vi)
             + jnp.einsum('bhtk,bhkv->bhtv', qi * jnp.exp(cum), s))
        k_tail = ki * jnp.exp(last - cum)
        s_new = jnp.exp(last)[:, :, 0, :, None] * s + jnp.einsum('bhsk,bhsv->bhkv', k_tail, vi)
        return s_new, o

    s_fin, oc = lax.scan(step, s0.astype(F32), (qc, kc, vc, gc))
    o = oc.transpose(1, 0, 3, 2, 4).reshape(b, t, h, -1)
    return o.astype(out_dtype), s_fin

def reverse_gated_scan(q, k, v, log_g, s0, chunk):
    o, s = chunked_gated_scan(*(jnp.flip(a, axis=1) for a in (q, k, v, log_g)), s0, chunk)
    return jnp.flip(o, axis=1), s

def context_attention(q, k, v, sink):
    b, l = q.shape[:2]
    qg = q.reshape(b, l, N_KV_HEADS, GQA_GROUP, HEAD_DIM)
    s = jnp.einsum('bqkgd,bckd->bkgqc', qg, k).astype(F32) * HEAD_DIM ** -0.5
    s_sink = jnp.broadcast_to(sink.astype(F32).reshape(1, N_KV_HEADS, GQA_GROUP, 1, 1),
                              (b, N_KV_HEADS, GQA_GROUP, l, 1))
    p = jax.nn.softmax(jnp.concatenate([s_sink, s], axis=-1), axis=-1)[..., 1:]
    o = jnp.einsum('bkgqc,bckd->bqkgd', p.astype(v.dtype), v)
    return o.reshape(b, l, N_Q_HEADS * HEAD_DIM)

def latent_attention(q, k, v, k_ctx, v_ctx, sink):
    b, t = q.shape[:2]
    nb = t // ATTN_BLOCK
    lc = k_ctx.shape[1]
    qb = q.reshape(b, nb, ATTN_BLOCK, N_KV_HEADS, GQA_GROUP, HEAD_DIM)

    def band(a):
        ap = jnp.pad(a, ((0, 0), (ATTN_BLOCK, ATTN_BLOCK), (0, 0), (0, 0)))
        ap = ap.reshape(b, nb + 2, ATTN_BLOCK, N_KV_HEADS, HEAD_DIM)
        return jnp.concatenate([ap[:, :-2], ap[:, 1:-1], ap[:, 2:]], axis=2)

    kb, vb = band(k), band(v)
    blk = jnp.arange(nb)[:, None, None] * ATTN_BLOCK
    qpos = blk + jnp.arange(ATTN_BLOCK)[None, :, None]
    kpos = blk - ATTN_BLOCK + jnp.arange(3 * ATTN_BLOCK)[None, None, :]
    valid = (jnp.abs(qpos - kpos) <= WINDOW) & (kpos >= 0) & (kpos < t)
    scale = HEAD_DIM ** -0.5
    s_loc = jnp.einsum('bnqkgd,bnrkd->bnkgqr', qb, kb).astype(F32) * scale
    s_loc = jnp.where(valid[None, :, None, None], s_loc, NEG_BIG)
    s_ctx = jnp.einsum('bnqkgd,bckd->bnkgqc', qb, k_ctx).astype(F32) * scale
    s_sink = jnp.broadcast_to(sink.astype(F32).reshape(1, 1, N_KV_HEADS, GQA_GROUP, 1, 1),
                              (b, nb, N_KV_HEADS, GQA_GROUP, ATTN_BLOCK, 1))
    p = jax.nn.softmax(jnp.concatenate([s_sink, s_ctx, s_loc], axis=-1), axis=-1)
    p_ctx = p[..., 1:1 + lc].astype(v.dtype)
    p_loc = p[..., 1 + lc:].astype(v.dtype)
    o = (jnp.einsum('bnkgqc,bckd->bnqkgd', p_ctx, v_ctx.astype(v.dtype))
         + jnp.einsum('bnkgqr,bnrkd->bnqkgd', p_loc, vb))
    return o.reshape(b, t, N_Q_HEADS * HEAD_DIM)

def even_mixer(h, P, j, ctx):
    b, t, _ = h.shape
    q, k, v, z, xbc, dt = jnp.split(h @ P['e_w_in'][j], EVEN_SPLITS, axis=-1)
    q = rms_norm(q.reshape(b, t, N_Q_HEADS, HEAD_DIM), P['e_q_norm'][j])
    k = rms_norm(k.reshape(b, t, N_KV_HEADS, HEAD_DIM), P['e_k_norm'][j])
    v = v.reshape(b, t, N_KV_HEADS, HEAD_DIM)
    xbc = jax.nn.silu(depthwise_conv(xbc, P['e_conv_w'][j], P['e_conv_b'][j]))
    xs, bm, cm = jnp.split(xbc, (SSD_D_INNER, SSD_D_INNER + SSD_GROUPS * D_STATE), axis=-1)
    xs = xs.reshape(b, t, SSD_HEADS, SSD_HEAD_DIM)
    rep = SSD_HEADS // SSD_GROUPS
    bm = jnp.repeat(bm.reshape(b, t, SSD_GROUPS, D_STATE), rep, axis=2)
    cm = jnp.repeat(cm.reshape(b, t, SSD_GROUPS, D_STATE), rep, axis=2)
    dt = jax.nn.softplus(dt.astype(F32).reshape(b, t, 2, SSD_HEADS) + P['e_dt_bias'][j].astype(F32))
    log_a = dt * -jnp.exp(P['e_a_log'][j].astype(F32))
    if ctx is None:
        s0 = jnp.zeros((b, 2, SSD_HEADS, D_STATE, SSD_HEAD_DIM), F32)
    else:
        s0 = ctx[2]
    y_f, s_f = chunked_gated_scan(cm, bm * dt[:, :, 0, :, None], xs, log_a[:, :, 0, :, None], s0[:, 0], SSD_CHUNK)
    y_b, s_b = reverse_gated_scan(cm, bm * dt[:, :, 1, :, None], xs, log_a[:, :, 1, :, None], s0[:, 1], SSD_CHUNK)
    y = y_f + y_b + P['e_d_skip'][j][:, None].astype(xs.dtype) * xs
    y = rms_norm(y.reshape(b, t, SSD_D_INNER) * jax.nn.silu(z), P['e_ssd_norm'][j])
    if ctx is None:
        o_attn = context_attention(q, k, v, P['e_sink'][j])
        new = (k, v, jnp.stack([s_f, s_b], axis=1))
    else:
        o_attn = latent_attention(axial_rope(q), axial_rope(k), v, ctx[0], ctx[1], P['e_sink'][j])
        new = None
    mix = jnp.concatenate([o_attn, y.astype(o_attn.dtype)], axis=-1)
    return mix @ P['e_w_out'][j], new

def hgrn_lower_bounds(lb_param):
    sm = jax.nn.softmax(lb_param.astype(F32), axis=0)
    return jnp.cumsum(sm, axis=0) - sm[:1]

def odd_mixer(h, P, j, lb, state0):
    b, t, _ = h.shape
    q, f_fw, f_bw, i, g = jnp.split(h @ P['o_w_in'][j], HGRN_SPLITS, axis=-1)
    q = (jax.nn.silu(q) * HGRN_DK ** -0.5).reshape(b, t, HGRN_HEADS, HGRN_DK)
    i = i.reshape(b, t, HGRN_HEADS, HGRN_DV)

    def gate(f, lb_d):
        f = f.astype(F32).reshape(b, t, HGRN_HEADS, HGRN_DK)
        lb_d = lb_d.reshape(HGRN_HEADS, HGRN_DK)
        forget = lb_d + (1.0 - lb_d) * jax.nn.sigmoid(f)
        return (1.0 - lb_d) * jax.nn.sigmoid(-f), jnp.log(forget)

    k_fw, lf_fw = gate(f_fw, lb[j, 0])
    k_bw, lf_bw = gate(f_bw, lb[j, 1])
    if state0 is None:
        state0 = jnp.zeros((b, 2, HGRN_HEADS, HGRN_DK, HGRN_DV), F32)
    o_fw, s_fw = chunked_gated_scan(q, k_fw, i, lf_fw, state0[:, 0], HGRN_CHUNK)
    o_bw, s_bw = reverse_gated_scan(q, k_bw, i, lf_bw, state0[:, 1], HGRN_CHUNK)
    g = g.reshape(b, t, HGRN_HEADS, HGRN_DV)
    o = rms_norm(o_fw + o_bw, P['o_g_norm'][j]) * jax.nn.silu(g)
    return o.reshape(b, t, HGRN_VW) @ P['o_w_out'][j], jnp.stack([s_fw, s_bw], axis=1)

def peer(h, P, l):
    b, t, d = h.shape
    m = b * t
    x = h.reshape(m, d)
    q = (x @ P['p_w_q'][l]).reshape(m, PEER_HEADS, 2, PEER_DKEY)
    s = jnp.einsum('mhpd,hpnd->mhpn', q, P['p_sub_keys'][l]).astype(F32)
    top_s, top_i = lax.top_k(s, PEER_TOPK)
    n_cand = PEER_TOPK * PEER_TOPK
    cand_s = (top_s[:, :, 0, :, None] + top_s[:, :, 1, None, :]).reshape(m, PEER_HEADS, n_cand)
    cand_e = (top_i[:, :, 0, :, None] * PEER_NKEYS + top_i[:, :, 1, None, :]).reshape(m, PEER_HEADS, n_cand)
    best_s, best_pos = lax.top_k(cand_s, PEER_TOPK)
    expert = jnp.take_along_axis(cand_e, best_pos, axis=-1)
    gate = jax.nn.softmax(best_s, axis=-1)
    u, v = P['p_u'][l], P['p_v'][l]

    def block(args):
        xb, eb, gb = args
        act = jax.nn.gelu(jnp.einsum('pd,phkd->phk', xb, u[eb]).astype(F32)) * gb
        return jnp.einsum('phk,phkd->pd', act.astype(xb.dtype), v[eb])

    nblk = m // PEER_BLOCK
    out = lax.map(block, (x.reshape(nblk, PEER_BLOCK, d),
                          expert.reshape(nblk, PEER_BLOCK, PEER_HEADS, PEER_TOPK),
                          gate.reshape(nblk, PEER_BLOCK, PEER_HEADS, PEER_TOPK)))
    return out.reshape(b, t, d)

def run_trunk(x, cond, P, cache):
    lb = hgrn_lower_bounds(P['o_lb'])
    ks, vs, ssd_states, hgrn_states = [], [], [], []
    for l in range(DEPTH):
        j = l // 2
        sh1, sc1, g1, sh2, sc2, g2 = modulation(cond, P['w_ada'][l], P['b_ada'][l])
        h = rms_norm(x, P['norm_mix'][l]) * (1 + sc1) + sh1
        if l % 2 == 0:
            ctx = None if cache is None else (cache[0][:, j], cache[1][:, j], cache[2][:, j])
            out, new = even_mixer(h, P, j, ctx)
            if cache is None:
                ks.append(new[0])
                vs.append(new[1])
                ssd_states.append(new[2])
        else:
            s0 = None if cache is None else cache[3][:, j]
            out, s_new = odd_mixer(h, P, j, lb, s0)
            if cache is None:
                hgrn_states.append(s_new)
        x = x + g1 * out
        h = rms_norm(x, P['norm_ffn'][l]) * (1 + sc2) + sh2
        x = x + g2 * peer(h, P, l)
    if cache is not None:
        return x, None
    return x, (jnp.stack(ks, axis=1), jnp.stack(vs, axis=1),
               jnp.stack(ssd_states, axis=1), jnp.stack(hgrn_states, axis=1))

def setup_inputs(seed: int = 0) -> dict:
    key = jax.random.key(seed)
    keys = iter(jax.random.split(key, 40))

    def nrm(shape, scale):
        return jax.random.normal(next(keys), shape, F32) * scale

    def gain(shape):
        return 1.0 + nrm(shape, 0.02)

    dt0 = jnp.exp(jax.random.uniform(next(keys), (N_EVEN, 2, SSD_HEADS), F32,
                                     math.log(1e-3), math.log(1e-1)))
    a_init = jax.random.uniform(next(keys), (N_EVEN, 2, SSD_HEADS), F32, 1.0, 16.0)
    return {
        'x_prompt': nrm((BATCH, SEQ, D_MODEL), 1.0),
        'x_sample': nrm((DEC_BATCH, DEC_SEQ, D_MODEL), 1.0),
        'cache_k': nrm((DEC_BATCH, N_EVEN, PAST_LEN, N_KV_HEADS, HEAD_DIM), 1.0),
        'cache_v': nrm((DEC_BATCH, N_EVEN, PAST_LEN, N_KV_HEADS, HEAD_DIM), 1.0),
        'state_ssd': nrm((DEC_BATCH, N_EVEN, 2, SSD_HEADS, D_STATE, SSD_HEAD_DIM), 0.5),
        'state_hgrn': nrm((DEC_BATCH, N_ODD, 2, HGRN_HEADS, HGRN_DK, HGRN_DV), 0.5),
        'c': nrm((DEC_BATCH, D_MODEL), 1.0),
        'c_ctx': nrm((D_MODEL,), 1.0),
        'w_ada': nrm((DEPTH, D_MODEL, 6 * D_MODEL), 0.5 * D_MODEL ** -0.5),
        'b_ada': nrm((DEPTH, 6 * D_MODEL), 0.02),
        'norm_mix': gain((DEPTH, D_MODEL)),
        'norm_ffn': gain((DEPTH, D_MODEL)),
        'e_w_in': nrm((N_EVEN, D_MODEL, EVEN_IN), D_MODEL ** -0.5),
        'e_q_norm': gain((N_EVEN, HEAD_DIM)),
        'e_k_norm': gain((N_EVEN, HEAD_DIM)),
        'e_sink': nrm((N_EVEN, N_Q_HEADS), 0.5),
        'e_conv_w': nrm((N_EVEN, CONV_K, SSD_CONV_DIM), CONV_K ** -0.5),
        'e_conv_b': nrm((N_EVEN, SSD_CONV_DIM), 0.02),
        'e_dt_bias': dt0 + jnp.log(-jnp.expm1(-dt0)),
        'e_a_log': jnp.log(a_init),
        'e_d_skip': gain((N_EVEN, SSD_HEADS)),
        'e_ssd_norm': gain((N_EVEN, SSD_D_INNER)),
        'e_w_out': nrm((N_EVEN, EVEN_MIX, D_MODEL), EVEN_MIX ** -0.5),
        'o_w_in': nrm((N_ODD, D_MODEL, HGRN_IN), D_MODEL ** -0.5),
        'o_lb': nrm((N_ODD, 2, HGRN_KW), 1.0),
        'o_g_norm': gain((N_ODD, HGRN_DV)),
        'o_w_out': nrm((N_ODD, HGRN_VW, D_MODEL), HGRN_VW ** -0.5),
        'p_w_q': nrm((DEPTH, D_MODEL, PEER_HEADS * 2 * PEER_DKEY), D_MODEL ** -0.5),
        'p_sub_keys': nrm((DEPTH, PEER_HEADS, 2, PEER_NKEYS, PEER_DKEY), PEER_DKEY ** -0.5),
        'p_u': nrm((DEPTH, PEER_EXPERTS, D_MODEL), D_MODEL ** -0.5),
        'p_v': nrm((DEPTH, PEER_EXPERTS, D_MODEL), PEER_HEADS ** -0.5),
    }

def reference(x_prompt, x_sample, cache_k, cache_v, state_ssd, state_hgrn, c, c_ctx,
              w_ada, b_ada, norm_mix, norm_ffn,
              e_w_in, e_q_norm, e_k_norm, e_sink, e_conv_w, e_conv_b, e_dt_bias, e_a_log,
              e_d_skip, e_ssd_norm, e_w_out,
              o_w_in, o_lb, o_g_norm, o_w_out,
              p_w_q, p_sub_keys, p_u, p_v):
    P = {
        'w_ada': w_ada, 'b_ada': b_ada, 'norm_mix': norm_mix, 'norm_ffn': norm_ffn,
        'e_w_in': e_w_in, 'e_q_norm': e_q_norm, 'e_k_norm': e_k_norm, 'e_sink': e_sink,
        'e_conv_w': e_conv_w, 'e_conv_b': e_conv_b, 'e_dt_bias': e_dt_bias, 'e_a_log': e_a_log,
        'e_d_skip': e_d_skip, 'e_ssd_norm': e_ssd_norm, 'e_w_out': e_w_out,
        'o_w_in': o_w_in, 'o_lb': o_lb, 'o_g_norm': o_g_norm, 'o_w_out': o_w_out,
        'p_w_q': p_w_q, 'p_sub_keys': p_sub_keys, 'p_u': p_u, 'p_v': p_v,
    }
    y_prompt, new_state = run_trunk(x_prompt, c_ctx[None, :], P, None)
    new_cache_k, new_cache_v, new_state_ssd, new_state_hgrn = new_state
    y_sample, _ = run_trunk(x_sample, c, P, (cache_k, cache_v, state_ssd, state_hgrn))
    return (y_prompt, y_sample, new_cache_k, new_cache_v, new_state_ssd, new_state_hgrn)


_drawn_inputs = setup_inputs


def setup_inputs(seed=0):
    import zlib

    import numpy as np

    out = dict(_drawn_inputs(seed))
    spreads = {}
    factors = {'cache_k': 4.744,
     'cache_v': 4.0,
     'state_hgrn': 8.0,
     'norm_ffn': 4.885,
     'e_q_norm': 8.0,
     'e_sink': 64.0,
     'e_d_skip': 24.73,
     'e_ssd_norm': 8.0,
     'o_g_norm': 32.363}
    for name, (base, spread) in spreads.items():
        noise = np.random.default_rng([zlib.crc32(name.encode()), seed]).standard_normal(out[name].shape)
        drawn = base * np.exp(spread * noise) if base else spread * noise
        out[name] = __import__('jax').numpy.asarray(drawn.astype(out[name].dtype))
    for name, factor in factors.items():
        out[name] = (out[name] * factor).astype(out[name].dtype)
    return out
```

```python
from contextlib import ExitStack

import numpy as np
import concourse.bass as bass
from concourse import mybir

F32 = mybir.dt.float32
U32 = mybir.dt.uint32
ALU = mybir.AluOpType
ACT = mybir.ActivationFunctionType
AX = mybir.AxisListType

P = 128
D = 1024
KC = D // P
TILES = 5
TOK = TILES * P
LAT = TOK - P
EPS = 1e-6
DEPTH = 2
PH, NK, TOPK = 8, 128, 16
SLOTS = PH * TOPK
RING = 8
DIAGS = 4
GELU_C = 0.7978845608028654
LOWEST = -3.0e38
EXP_LN = "natural_log_exp_and_others"


class Sem:

    def __init__(self, handle):
        self.h, self.base = handle, 0

    def at(self, n):
        return n + self.base


class Chain:

    def __init__(self, eng, sem):
        self.eng, self.sem, self.n, self.k = eng, sem, sem.base, 0

    def __call__(self, ins):
        ins.then_inc(self.sem.h, 1)
        self.n = self.n + 1
        self.k += 1
        self.eng.wait_ge(self.sem.h, self.n)
        self.eng.nop(nofuse=True)

    def enter(self, i, per):
        self.start, self.per = self.n, per
        self.n = i * per + self.start

    def leave(self, count):
        self.n = self.start + count * self.per

    def close(self):
        self.sem.base = self.n


def cond_of(t):
    return 0 if t == 0 else 1


class Names:
    pass


def fresh(nc, m, names, tag):
    return [Sem(m.ctx.enter_context(nc.semaphore(f"s_{tag}_{n}"))) for n in names.split()]


def setup_phase(nc, m):
    s = m.sems
    with nc.Block() as block:
        @block.sync
        def _(sp):
            sp.dma_start(m.condr[0:KC, :], m.c_ctx.rearrange("(k p) -> k p", p=P)).then_inc(s.cond.h, 16)
            sp.dma_start(m.condr[KC:2 * KC, :], m.c.rearrange("o (k p) -> (o k) p", p=P)).then_inc(s.cond.h, 16)
            sp.dma_start(m.ident[:, :], m.c_ident).then_inc(s.cond.h, 16)
            for l in range(DEPTH):
                w = m.w_ada[l].rearrange("(k p) n -> p k n", p=P)
                for b in range(4):
                    if l > 0:
                        sp.wait_ge(s.mp.h, s.mp.at(12 * l - 3 + b))
                    sp.dma_start(m.wa[:, b, :, :], w[:, :, b * 512:(b + 1) * 512]).then_inc(s.wq[b].h, 16)
                with sp.Fori(1, 3) as i:
                    for b in range(4):
                        sp.wait_ge(s.mp.h, 4 * i + s.mp.at(12 * l + b - 3))
                        sp.dma_start(m.wa[:, b, :, :], w[:, :, bass.ds(i * 2048 + b * 512, 512)]).then_inc(s.wq[b].h, 16)
            sp.wait_ge(s.mrow.h, s.mrow.at(4 * DEPTH))
            for l in range(DEPTH):
                for j in range(6):
                    src = (1, 0, 2, 4, 3, 5)[j]
                    sp.dma_start(m.mod.rearrange("(l c j) d -> l j c d", l=DEPTH, c=2)[l, j], m.mrow[0:2, l, src * D:(src + 1) * D]).then_inc(s.modst.h, 16)
            sp.wait_ge(s.modst.h, s.modst.at(16 * 12))

        @block.gpsimd
        def _(pool):
            for (dst, src) in m.const_loads:
                pool.dma_start(dst, src).then_inc(s.const.h, 16)
            for l in range(DEPTH):
                pool.dma_start(m.brow[0:2, l, :], m.b_ada[l:l + 1, :].to_broadcast([2, 6 * D])).then_inc(s.const.h, 16)
                for j in range(2):
                    src = (m.norm_mix, m.norm_ffn)[j]
                    pool.dma_start(m.nrow[l][0:2, j, :], src[l:l + 1, :].to_broadcast([2, D])).then_inc(s.const.h, 16)
            pool.dma_start(m.x[:, 0, :], m.x_prompt[0]).then_inc(s.const.h, 16)
            pool.dma_start(m.x[:, 1:, :], m.x_sample[0].rearrange("(t p) d -> p t d", p=P)).then_inc(s.const.h, 16)
            pool.wait_ge(s.const.h, s.const.at(m.n_const))

        @block.tensor
        def _(pe):
            pe.wait_ge(s.cond.h, s.cond.at(48))
            nc.tensor.transpose(m.ps[7][:, 0:16], m.condr[:, :], m.ident[0:16, 0:16]).then_inc(s.condt.h, 1)
            pe.wait_ge(s.condr.h, s.condr.at(1))
            for l in range(DEPTH):
                with pe.Fori(0, 3) as i:
                    for b in range(4):
                        pe.wait_ge(s.wq[b].h, 16 * i + s.wq[b].at(48 * l + 16))
                        pe.wait_ge(s.mc.h, 4 * i + s.mc.at(12 * l + b + 1))
                        for k in range(KC):
                            q = nc.tensor.matmul(m.ps[b][0:2, :], m.condT[:, k, :], m.wa[:, b, k, :], start=(k == 0), stop=(k == KC - 1))
                        q.then_inc(s.mp.h, 1)

        @block.scalar
        def _(act):
            nc.scalar.preload_act_table_set(EXP_LN)
            act.wait_ge(s.condm.h, s.condm.at(1))
            nc.scalar.activation(m.ce[:, :], m.ce[:, :], ACT.Exp, scale=-1.0).then_inc(s.ce.h, 1)

        @block.vector
        def _(dve):
            ch = Chain(dve, s.cv)
            ch(nc.vector.memset(m.zeros[:, :], 0.0))
            dve.wait_ge(s.condt.h, s.condt.at(1))
            nc.vector.tensor_scalar(m.ce[:, :], m.ps[7][:, 0:16], -80.0, None, ALU.max).then_inc(s.condm.h, 1)
            dve.wait_ge(s.ce.h, s.ce.at(1))
            ch(nc.vector.tensor_scalar(m.ce[:, :], m.ce[:, :], 1.0, None, ALU.add))
            ch(nc.vector.reciprocal(m.ce[:, :], m.ce[:, :]))
            nc.vector.tensor_tensor(m.condT[:, :, :].rearrange("p k c -> p c k"), m.ce[:, :].rearrange("p (c k) -> p c k", c=2),
                                    m.ps[7][:, 0:16].rearrange("p (c k) -> p c k", c=2), ALU.mult).then_inc(s.condr.h, 1)
            nc.vector.memset(m.zeros[0:1, 0:1], 0.0).then_inc(s.mc.h, 4)
            dve.wait_ge(s.const.h, s.const.at(m.n_const))
            for l in range(DEPTH):
                with dve.Fori(0, 3) as i:
                    for b in range(4):
                        dve.wait_ge(s.mp.h, 4 * i + s.mp.at(12 * l + b + 1))
                        nc.vector.tensor_tensor(m.mrow[0:2, l, bass.ds(i * 2048 + b * 512, 512)], m.ps[b][0:2, :],
                                                m.brow[0:2, l, bass.ds(i * 2048 + b * 512, 512)], ALU.add).then_inc(s.mc.h, 1)
                dve.wait_ge(s.mc.h, s.mc.at(12 * l + 16))
                for j in range(2):
                    a = m.mrow[0:2, l, (3 * j + 1) * D:(3 * j + 2) * D]
                    ch(nc.vector.tensor_scalar(a, a, 1.0, None, ALU.add))
                    nc.vector.tensor_tensor(a, a, m.nrow[l][0:2, j, :], ALU.mult).then_inc(s.mrow.h, 2)
            ch.close()
    for b in range(4):
        s.wq[b].base += 48 * DEPTH


def norm_phase(nc, m, l, which, prefetch):
    s = m.sems
    row = l * 12 + which * 3
    bc, h, hT, x = m.bc, m.h, m.hT, m.x
    with nc.Block() as block:
        @block.sync
        def _(sp):
            for c in range(2):
                for k in range(2):
                    sp.dma_start(bc[:, c, k, :], m.mod[row + 6 * c + k:row + 6 * c + k + 1, :].to_broadcast([P, D])).then_inc(s.bc.h, 16)
                sp.dma_start(m.gate[:, c, :], m.mod[row + 6 * c + 2:row + 6 * c + 3, :].to_broadcast([P, D])).then_inc(s.bc.h, 16)
            prefetch(sp)
            sp.wait_ge(s.bc.h, s.bc.at(96))

        @block.scalar
        def _(act):
            ch = Chain(act, s.ca)
            for t in range(TILES):
                ch(nc.scalar.activation(m.junk[:, :], x[:, t, :], ACT.Square, accum_out=m.ss[:, t:t + 1]))
                ch(nc.scalar.activation(m.ss[:, t:t + 1], m.ss[:, t:t + 1], ACT.Ln, scale=1.0 / D, bias=m.eps[:, 0:1]))
                nc.scalar.activation(m.rs[:, t:t + 1], m.ss[:, t:t + 1], ACT.Exp, scale=-0.5).then_inc(s.rs.h, 1)
            for t in range(TILES):
                act.wait_ge(s.tp.h, s.tp.at(t + 1))
                for b in range(2):
                    i = nc.scalar.activation(hT[:, 4 * b:4 * b + 4, t * P:(t + 1) * P],
                                             m.ps[2 * (t % 2) + b][:, :].rearrange("p (c t) -> p c t", c=4), ACT.Copy)
                i.then_inc(s.tpfree.h, 1)
            ch.close()

        @block.vector
        def _(dve):
            ch = Chain(dve, s.cv)
            dve.wait_ge(s.bc.h, s.bc.at(96))
            for t in range(TILES):
                c = cond_of(t)
                dve.wait_ge(s.rs.h, s.rs.at(t + 1))
                ch(nc.vector.scalar_tensor_tensor(out=h[:, t, :], in0=x[:, t, :], scalar=m.rs[:, t:t + 1],
                                                  in1=bc[:, c, 0, :], op0=ALU.mult, op1=ALU.mult))
                nc.vector.tensor_tensor(h[:, t, :], h[:, t, :], bc[:, c, 1, :], ALU.add).then_inc(s.hr.h, 1)
            ch.close()

        @block.tensor
        def _(pe):
            for t in range(TILES):
                pe.wait_ge(s.hr.h, s.hr.at(t + 1))
                if t >= 2:
                    pe.wait_ge(s.tpfree.h, s.tpfree.at(t - 1))
                for k in range(KC):
                    i = nc.tensor.transpose(m.ps[2 * (t % 2) + k // 4][:, (k % 4) * P:(k % 4 + 1) * P],
                                            h[:, t, k * P:(k + 1) * P], m.ident[:, :])
                i.then_inc(s.tp.h, 1)
    s.bc.base += 96
    for q in (s.rs, s.tp, s.tpfree, s.hr):
        q.base += TILES


TK = 21


def topk_head(nc, m, ch, l, tau, i):
    ch(nc.vector.tensor_copy(m.cs[:, :], m.S[:, tau, bass.ds(i * 2 * P, 2 * P)]))
    for p in range(2):
        a = m.cs[:, p * P:(p + 1) * P]
        ch(nc.vector.max(m.tv[:, p, 0:8], a))
        nc.vector.max_index(m.ti[:, p, 0:8], m.tv[:, p, 0:8], a)
        ch(nc.vector.match_replace(m.cs2[:, p * P:(p + 1) * P], m.tv[:, p, 0:8], a, LOWEST))
        ch(nc.vector.max(m.tv[:, p, 8:16], m.cs2[:, p * P:(p + 1) * P]))
        ch(nc.vector.max_index(m.ti[:, p, 8:16], m.tv[:, p, 8:16], m.cs2[:, p * P:(p + 1) * P]))
    nc.vector.tensor_copy(m.tif[:, :, :], m.ti[:, :, :])
    ch(nc.vector.tensor_tensor(m.cs[:, :].rearrange("p (a b) -> p a b", a=TOPK),
                               m.tv[:, 0, :].unsqueeze(2).to_broadcast([P, TOPK, TOPK]),
                               m.tv[:, 1, :].unsqueeze(1).to_broadcast([P, TOPK, TOPK]), ALU.add))
    ch(nc.vector.max(m.bv[:, 0:8], m.cs[:, :]))
    nc.vector.max_index(m.bp[:, 0:8], m.bv[:, 0:8], m.cs[:, :])
    ch(nc.vector.match_replace(m.cs2[:, :], m.bv[:, 0:8], m.cs[:, :], LOWEST))
    ch(nc.vector.max(m.bv[:, 8:16], m.cs2[:, :]))
    ch(nc.vector.max_index(m.bp[:, 8:16], m.bv[:, 8:16], m.cs2[:, :]))
    nc.vector.tensor_copy(m.bs[:, tau % 2, bass.ds(i * TOPK, TOPK)], m.bv[:, :])
    nc.vector.tensor_single_scalar(m.pi[:, 0, :], m.bp[:, :], 4, ALU.logical_shift_right)
    ch(nc.vector.tensor_single_scalar(m.pi[:, 1, :], m.bp[:, :], TOPK - 1, ALU.bitwise_and))
    ch(nc.vector.tensor_copy(m.pf[:, :, :], m.pi[:, :, :]))
    ch(nc.vector.tensor_tensor(m.oh[:, :, :], m.pf[:, :, :].rearrange("p a b -> p (a b)").unsqueeze(2).to_broadcast([P, 2 * TOPK, TOPK]),
                               m.iota[:, :].unsqueeze(1).to_broadcast([P, 2 * TOPK, TOPK]), ALU.is_equal))
    for p in range(2):
        q = nc.vector.tensor_tensor(m.oh[:, p * TOPK:(p + 1) * TOPK, :], m.oh[:, p * TOPK:(p + 1) * TOPK, :],
                                    m.tif[:, p, :].unsqueeze(1).to_broadcast([P, TOPK, TOPK]), ALU.mult)
    ch(q)
    ch(nc.vector.tensor_reduce(m.ek[:, :], m.oh[:, :, :], AX.X, ALU.add))
    ch(nc.vector.scalar_tensor_tensor(out=m.ef[:, :], in0=m.ek[:, 0:TOPK], scalar=float(NK), in1=m.ek[:, TOPK:], op0=ALU.mult, op1=ALU.add))
    ch(nc.vector.tensor_scalar(m.idx[:, tau % 3, bass.ds(i * TOPK, TOPK)], m.ef[:, :], float(l * NK * NK), None, ALU.add))


def router_phase(nc, m, l):
    s = m.sems
    w_q = m.p_w_q[l].rearrange("(k p) n -> p k n", p=P)
    keys = m.p_sub_keys[l].rearrange("h s n d -> n (h s) d")

    def first_weights(sp):
        sp.dma_start(m.keys[:, :, :], keys).then_inc(s.keys.h, 16)
        for b in range(2):
            sp.dma_start(m.wq[:, b, :, :], w_q[:, :, b * 256:(b + 1) * 256]).then_inc(s.wq[b].h, 16)

    norm_phase(nc, m, l, 1, first_weights)
    with nc.Block() as block:
        @block.sync
        def _(sp):
            with sp.Fori(1, PH // 2) as i:
                for b in range(2):
                    sp.wait_ge(s.qp.h, 4 * i + s.qp.at(2 * b - 2))
                    sp.dma_start(m.wq[:, b, :, :], w_q[:, :, bass.ds(i * 512 + b * 256, 256)]).then_inc(s.wq[b].h, 16)
            for b in range(2):
                sp.wait_ge(s.wq[b].h, s.wq[b].at(16 * PH // 2))

        @block.tensor
        def _(pe):
            pe.wait_ge(s.keys.h, s.keys.at(16))
            for g in range(4):
                for k in range(4):
                    i = nc.tensor.transpose(m.ps[g][:, k * P:(k + 1) * P], m.keys[:, 4 * g + k, :], m.ident[:, :])
                i.then_inc(s.kt.h, 1)
            pe.wait_ge(s.ktc.h, s.ktc.at(4))
            with pe.Fori(0, PH // 2) as i:
                for b in range(2):
                    n = 2 * i + b
                    pe.wait_ge(s.wq[b].h, 16 * i + s.wq[b].at(16))
                    for side in range(2):
                        pe.wait_ge(s.qc.h, 2 * n + s.qc.at(side + 1))
                        for (bank, lo, w) in ((2 * side, P, LAT), (2 * side + 1, 0, P)):
                            for k in range(KC):
                                mm = nc.tensor.matmul(m.ps[bank][:, 0:w], m.wq[:, b, k, side * P:(side + 1) * P],
                                                      m.hT[:, k, lo:lo + w], start=(k == 0), stop=(k == KC - 1))
                        mm.then_inc(s.qp.h, 1)
                    for side in range(2):
                        pe.wait_ge(s.qc.h, 2 * n + s.qc.at(side + 3))
                        pe.wait_ge(s.sc.h, 2 * n + s.sc.at(side + 1))
                        for t in range(TILES):
                            o = m.ps[5 + 2 * side][:, 0:P] if t == 0 else m.ps[4 + 2 * side][:, (t - 1) * P:t * P]
                            mm = nc.tensor.matmul(o, m.qT[:, side, t * P:(t + 1) * P],
                                                  m.keysT[:, bass.ds(n * 2 * P + side * P, P)], start=True, stop=True)
                        mm.then_inc(s.spd.h, 1)

        @block.scalar
        def _(act):
            for g in range(4):
                act.wait_ge(s.kt.h, s.kt.at(g + 1))
                nc.scalar.activation(m.keysT[:, 4 * g * P:(4 * g + 4) * P], m.ps[g][:, :], ACT.Copy).then_inc(s.ktc.h, 1)
            nc.scalar.activation(m.junk[:, 0:1], m.eps[:, 0:1], ACT.Copy).then_inc(s.qc.h, 2)
            with act.Fori(0, PH // 2) as i:
                for b in range(2):
                    for side in range(2):
                        act.wait_ge(s.qp.h, 4 * i + s.qp.at(2 * b + side + 1))
                        nc.scalar.activation(m.qT[:, side, P:], m.ps[2 * side][:, :], ACT.Copy)
                        nc.scalar.activation(m.qT[:, side, 0:P], m.ps[2 * side + 1][:, 0:P], ACT.Copy).then_inc(s.qc.h, 1)

        @block.vector
        def _(dve):
            ch = Chain(dve, s.cv)
            nc.vector.memset(m.ss[:, 0:1], 0.0).then_inc(s.sc.h, 2)
            with dve.Fori(0, PH // 2) as i:
                ch.enter(i, 2 * TK)
                for b in range(2):
                    for side in range(2):
                        dve.wait_ge(s.spd.h, 4 * i + s.spd.at(2 * b + side + 1))
                        g = 4 * i + (2 * b + side)
                        nc.vector.tensor_copy(m.S[:, 1:TILES, bass.ds(g * P, P)],
                                              m.ps[4 + 2 * side][:, :].rearrange("p (t n) -> p t n", t=4))
                        nc.vector.tensor_copy(m.S[:, 0, bass.ds(g * P, P)], m.ps[5 + 2 * side][:, 0:P]).then_inc(s.sc.h, 1)
                    dve.wait_ge(s.sc.h, 4 * i + s.sc.at(2 * b + 4))
                    dve.nop(nofuse=True)
                    topk_head(nc, m, ch, l, 0, 2 * i + b)
            ch.leave(PH // 2)
            ch.close()
    for b in range(2):
        s.wq[b].base += 16 * PH // 2
    s.keys.base += 16
    s.kt.base += 4
    s.ktc.base += 4
    s.qp.base += 2 * PH
    s.spd.base += 2 * PH
    s.qc.base += 2 * PH + 2
    s.sc.base += 2 * PH + 2


def gather_phase(nc, m, l):
    s = m.sems
    u_flat, v_flat = m.p_u.rearrange("l e d -> (l e) d"), m.p_v.rearrange("l e d -> (l e) d")
    x = m.x

    with nc.Block() as block:
        @block.gpsimd
        def _(pool):
            for st in range(TILES + 1):
                do_u, do_v = st < TILES, st >= 1
                if do_u:
                    pool.wait_ge(s.ix.h, s.ix.at(st + 1))
                with pool.Fori(0, PH) as i:
                    n = do_u + do_v
                    done = sum(((q < TILES) + (q >= 1)) * PH * 2 for q in range(st))
                    for j in range(TOPK):
                        b = j % RING
                        if b == 0:
                            if do_u:
                                nc.gpsimd.tensor_copy(m.iu[:, j:j + RING], m.idx[:, st % 3, bass.ds(i * TOPK + j, RING)]).then_inc(s.ist.h, 1)
                            if do_v:
                                nc.gpsimd.tensor_copy(m.iv[:, j:j + RING], m.idx[:, (st - 1) % 3, bass.ds(i * TOPK + j, RING)]).then_inc(s.ist.h, 1)
                            pool.wait_ge(s.ist.h, i * 2 * n + s.ist.at(done + n * (j // RING + 1)))
                        if do_u:
                            pool.wait_ge(s.ufree.h, i * TOPK + s.ufree.at(st * SLOTS + j + 1))
                            pool.nop(nofuse=True)
                            nc.gpsimd.indirect_dma_start(m.ur[:, b, :], None, u_flat, bass.IndirectOffsetOnAxis(ap=m.iu[:, j:j + 1], axis=0)).then_inc(s.ud[b].h, 16)
                        if do_v:
                            pool.wait_ge(s.vfree.h, i * TOPK + s.vfree.at((st - 1) * SLOTS + j + 1))
                            pool.nop(nofuse=True)
                            nc.gpsimd.indirect_dma_start(m.vr[:, b, :], None, v_flat, bass.IndirectOffsetOnAxis(ap=m.iv[:, j:j + 1], axis=0)).then_inc(s.vd[b].h, 16)

        @block.vector
        def _(dve):
            ch = Chain(dve, s.cv)
            nc.vector.memset(m.ss[:, 0:1], 0.0).then_inc(s.ufree.h, RING)
            nc.vector.tensor_copy(m.h2p[:, :], m.h[:, 0, :]).then_inc(s.ix.h, 1)
            for st in range(TILES + 1):
                if st < TILES:
                    do_k = st + 1 < TILES
                    base = ch.n
                    per = 1 + (TK if do_k else 0)
                    with dve.Fori(0, PH) as i:
                        for j in range(TOPK):
                            b = j % RING
                            dve.wait_ge(s.ud[b].h, 32 * i + s.ud[b].at(16 * (2 * PH * st + j // RING + 1)))
                            nc.vector.tensor_tensor_reduce(m.ur[:, b, :], m.ur[:, b, :], m.h2p[:, :], 1.0, 0.0,
                                                           ALU.mult, ALU.add, m.d16[:, j:j + 1]).then_inc(s.ufree.h, 1)
                        dve.wait_ge(s.ufree.h, TOPK * i + s.ufree.at(RING + SLOTS * st + TOPK))
                        ch.n = i * per + base
                        ch(nc.vector.tensor_copy(m.dots[:, bass.ds(i * TOPK, TOPK)], m.d16[:, :]))
                        if do_k:
                            topk_head(nc, m, ch, l, st + 1, i)
                    ch.n = base + per * PH
                    if do_k:
                        nc.vector.tensor_copy(m.h2p[:, :], m.h[:, st + 1, :]).then_inc(s.ix.h, 1)
                    bs = m.bs[:, st % 2, :].rearrange("p (h k) -> p h k", h=PH)
                    w3 = m.wt[:, st % 2, :].rearrange("p (h k) -> p h k", h=PH)
                    sm = m.sm[:, :].rearrange("p (h k) -> p h k", h=PH)
                    nc.vector.tensor_tensor(sm, bs, bs[:, :, 0:1].to_broadcast([P, PH, TOPK]), ALU.subtract).then_inc(s.smx.h, 1)
                    ch(nc.vector.tensor_tensor(m.gx[:, :], m.dots[:, :], m.dots[:, :], ALU.mult))
                    ch(nc.vector.tensor_scalar(m.gx[:, :], m.gx[:, :], 0.044715, 1.0, ALU.mult, ALU.add))
                    ch(nc.vector.tensor_tensor(m.gx[:, :], m.gx[:, :], m.dots[:, :], ALU.mult))
                    nc.vector.tensor_scalar(m.gx[:, :], m.gx[:, :], -50.0, None, ALU.max).then_inc(s.smx.h, 1)
                    dve.wait_ge(s.sme.h, s.sme.at(2 * st + 1))
                    ch(nc.vector.tensor_reduce(m.sr[:, :], sm, AX.X, ALU.add))
                    ch(nc.vector.reciprocal(m.sr[:, :], m.sr[:, :]))
                    ch(nc.vector.tensor_tensor(sm, sm, m.sr[:, :].unsqueeze(2).to_broadcast([P, PH, TOPK]), ALU.mult))
                    ch(nc.vector.tensor_tensor(m.sm[:, :], m.sm[:, :], m.dots[:, :], ALU.mult))
                    dve.wait_ge(s.sme.h, s.sme.at(2 * st + 2))
                    ch(nc.vector.tensor_scalar(m.gx[:, :], m.gx[:, :], 1.0, None, ALU.add))
                    ch(nc.vector.reciprocal(m.gx[:, :], m.gx[:, :]))
                    if st >= 2:
                        dve.wait_ge(s.dg.h, s.dg.at((st - 1) * SLOTS))
                    nc.vector.tensor_tensor(m.wt[:, st % 2, :], m.sm[:, :], m.gx[:, :], ALU.mult).then_inc(s.wr.h, 1)
                if st >= 2:
                    for t in ([st - 2] if st < TILES else [st - 2, st - 1]):
                        c = cond_of(t)
                        dve.wait_ge(s.acc.h, s.acc.at(t + 1))
                        ch(nc.vector.tensor_tensor(m.junk[:, :], m.acc[t % 2], m.gate[:, c, :], ALU.mult))
                        q = nc.vector.tensor_tensor(x[:, t, :], x[:, t, :], m.junk[:, :], ALU.add)
                        q.then_inc(s.accfree.h, 1)
                        dve.wait_ge(s.accfree.h, s.accfree.at(t + 1))
            ch.close()

        @block.scalar
        def _(act):
            for st in range(TILES + 1):
                if st >= 1:
                    act.wait_ge(s.wr.h, s.wr.at(st))
                    with act.Fori(0, PH) as i:
                        for j in range(TOPK):
                            act.wait_ge(s.vfree.h, i * TOPK + s.vfree.at((st - 1) * SLOTS + j + 1 + RING - DIAGS))
                            nc.scalar.activation(m.dgb[:, j % DIAGS, :], m.ident[:, :], ACT.Copy,
                                                 scale=m.wt[:, (st - 1) % 2, bass.ds(i * TOPK + j, 1)]).then_inc(s.dg.h, 1)
                if st < TILES:
                    act.wait_ge(s.smx.h, s.smx.at(2 * st + 1))
                    nc.scalar.activation(m.sm[:, :], m.sm[:, :], ACT.Exp).then_inc(s.sme.h, 1)
                    act.wait_ge(s.smx.h, s.smx.at(2 * st + 2))
                    nc.scalar.activation(m.gx[:, :], m.gx[:, :], ACT.Exp, scale=-2.0 * GELU_C).then_inc(s.sme.h, 1)

        @block.tensor
        def _(pe):
            for t in range(TILES):
                if t >= 2:
                    pe.wait_ge(s.accfree.h, s.accfree.at(t - 1))
                o = m.acc[t % 2]
                for b in range(2):
                    q = nc.tensor.matmul(o[:, b * 512:(b + 1) * 512], m.zeros[:, 0:P], m.zeros[:, 0:512], start=True, stop=False, skip_group_check=True)
                if t == 0:
                    q.then_inc(s.vfree.h, RING)
                with pe.Fori(0, PH) as i:
                    for j in range(TOPK):
                        b = j % RING
                        pe.wait_ge(s.dg.h, i * TOPK + s.dg.at(t * SLOTS + j + 1))
                        pe.wait_ge(s.vd[b].h, 32 * i + s.vd[b].at(16 * (2 * PH * t + j // RING + 1)))
                        for k in range(2):
                            q = nc.tensor.matmul(o[:, k * 512:(k + 1) * 512], m.dgb[:, j % DIAGS, :], m.vr[:, b, k * 512:(k + 1) * 512],
                                                 start=False, stop=False, skip_group_check=True)
                        q.then_inc(s.vfree.h, 1)
                for b in range(2):
                    q = nc.tensor.matmul(o[:, b * 512:(b + 1) * 512], m.zeros[:, 0:P], m.zeros[:, 0:512], start=False, stop=True, skip_group_check=True)
                q.then_inc(s.acc.h, 1)
    s.ix.base += TILES
    s.ist.base += 4 * TILES * PH
    s.ufree.base += RING + TILES * SLOTS
    s.vfree.base += RING + TILES * SLOTS
    for b in range(RING):
        s.ud[b].base += 16 * TILES * SLOTS // RING
        s.vd[b].base += 16 * TILES * SLOTS // RING
    s.smx.base += 2 * TILES
    s.sme.base += 2 * TILES
    s.wr.base += TILES
    s.dg.base += TILES * SLOTS
    s.acc.base += TILES
    s.accfree.base += TILES


HD, QH, KVH = 64, 8, 2
QKV = (QH + 2 * KVH) * HD
DI = 512
EC0, EZ0, EX0, ED0 = 0, QKV, QKV + DI, QKV + DI + DI + 256
SH = 8
XC = 6
CONV = 5
SPAN = 644


def off(t):
    return 0 if t == 0 else 132 + (t - 1) * P


def even_memory(nc, m, Arena):
    r = Arena()
    m.qkv = r.take(TILES, QKV)
    m.z = r.take(TILES, DI)
    m.dt = r.take(TILES, 16)
    xp = r.at
    m.xpad = r.take(XC, SPAN + 4)
    m.xc = r.take(XC, SPAN)
    m.mask = r.take(512)
    m.tri = r.take(4, P)
    assert r.at <= 15360
    r = Arena(xp)
    m.xs = r.take(TILES, DI)
    m.bmt = r.take(TILES, P)
    r = Arena(20480)
    st = r.at
    m.ew = r.take(2, KC, 512)
    m.qTz = r.take(QH, TOK)
    m.kTd = r.take(2, TOK + P)
    m.y = r.take(TILES, DI)
    m.oa = r.take(TILES, DI)
    m.cmz = r.take(2, SPAN)
    m.ckv = r.take(2, P)
    m.kd = r.take(2, 2 * P)
    m.kdc = r.take(2 * P)
    small = r.at
    m.bsink, m.bskip, m.balog, m.bdtb = r.take(QH), r.take(SH), r.take(16), r.take(16)
    m.bqk = r.take(2, HD)
    m.cwb = r.take(XC, CONV + 1)
    m.la = r.take(TILES, 16)
    m.c48, m.e48, m.wt48 = r.take(TILES, 48), r.take(TILES, 48), r.take(TILES, 16)
    m.r10 = r.take(TILES, 10)
    m.r10s = r.take(TILES, 10)
    m.mx, m.smx, m.sk = r.take(TILES, QH), r.take(TILES, QH), r.take(TILES, QH)
    q = Arena(st)
    m.cos, m.sin = q.take(4, HD), q.take(4, HD)
    m.t1, m.t2, m.t3 = q.take(2, 640), q.take(2, 640), q.take(2, 640)
    m.wrow = q.take(XC * P)[0:CONV + 1, :]
    q = Arena(st)
    m.seg = q.take(2, SH, P)
    m.cbm = q.take(2, 2, P)
    m.xw = q.take(2, DI)
    m.st = q.take(2, 4, HD)
    m.stc = q.take(2, 4, HD)
    m.yt = q.take(2, DI)
    m.bnorm = q.take(DI)
    m.pjunk = m.seg[:, 0, 0:4, :].rearrange("p h t -> p (h t)")
    q = Arena(st)
    m.pr = q.take(2, 512)
    m.pT = q.take(2, 512)
    m.mixT = m.hT


def even_project(nc, m):
    s = Names()
    (s.wA, s.wB, s.unit, s.evA, s.evV, s.pads) = fresh(nc, m, "wA wB unit evA evV pads", "ep")
    w = m.e_w_in[0].rearrange("(k p) n -> p k n", p=P)
    pieces = [(0, 512), (512, 256), (EZ0, DI), (ED0, 16), (EX0, 384), (EX0 + 384, 384)]
    units = []
    for p, (c0, width) in enumerate(pieces):
        if p < 4:
            units += [(p, "rows", t) for t in range(TILES)]
        else:
            units += [(p, k, c) for c in range(3) for k in ("lat", "ctx")]
    last_unit = [max(n for n, u in enumerate(units) if u[0] == p) + 1 for p in range(len(pieces))]

    def evacuate(eng, mine):
        for n, (p, kind, c) in enumerate(units):
            if n % 2 != mine:
                continue
            eng.wait_ge(s.unit.h, n + 1)
            ps = m.ps[n % 8]
            if kind == "rows":
                dst = {0: m.qkv[:, c, 0:512], 1: m.qkv[:, c, 512:768], 2: m.z[:, c, :], 3: m.dt[:, c, :]}[p]
                src = ps[:, 0:pieces[p][1]]
            else:
                ch = (p - 4) * 3 + c
                dst, src = (m.xpad[:, ch, 134:134 + LAT], ps[:, :]) if kind == "lat" else (m.xpad[:, ch, 2:2 + P], ps[:, 0:P])
            if mine == 0:
                nc.scalar.activation(dst, src, ACT.Copy).then_inc(s.evA.h, 1)
            else:
                nc.vector.tensor_copy(dst, src).then_inc(s.evV.h, 1)


    def load(sp, p):
        c0, width = pieces[p]
        sp.dma_start(m.ew[:, p % 2, :, 0:width], w[:, :, c0:c0 + width]).then_inc((s.wA, s.wB)[p % 2].h, 16)

    def first_weights(sp):
        load(sp, 0)
        load(sp, 1)

    norm_phase(nc, m, 0, 0, first_weights)
    with nc.Block() as block:
        @block.sync
        def _(sp):
            for p in range(2, len(pieces)):
                sp.wait_ge(s.unit.h, last_unit[p - 2])
                load(sp, p)
            sp.wait_ge(s.wA.h, 48)
            sp.wait_ge(s.wB.h, 48)

        @block.gpsimd
        def _(pool):
            for c in range(2):
                nc.gpsimd.memset(m.xpad[:, :, (0, 130)[c]:(2, 134)[c]], 0.0).then_inc(s.pads.h, 1)
            nc.gpsimd.memset(m.xpad[:, :, SPAN + 2:SPAN + 4], 0.0).then_inc(s.pads.h, 1)
            nc.gpsimd.memset(m.qTz[:, :, :], 0.0).then_inc(s.pads.h, 1)
            pool.wait_ge(s.pads.h, 4)

        @block.tensor
        def _(pe):
            for n, (p, kind, c) in enumerate(units):
                pe.wait_ge((s.wA, s.wB)[p % 2].h, 16 * (p // 2 + 1))
                if n >= 8:
                    pe.wait_ge((s.evA, s.evV)[n % 2].h, (n - 8) // 2 + 1)
                width = pieces[p][1]
                for k in range(KC):
                    if kind == "rows":
                        q = nc.tensor.matmul(m.ps[n % 8][:, 0:width], m.hT[:, k, c * P:(c + 1) * P], m.ew[:, p % 2, k, 0:width],
                                             start=(k == 0), stop=(k == KC - 1))
                    else:
                        lo, wd = (P, LAT) if kind == "lat" else (0, P)
                        q = nc.tensor.matmul(m.ps[n % 8][:, 0:wd], m.ew[:, p % 2, k, c * P:(c + 1) * P], m.hT[:, k, lo:lo + wd],
                                             start=(k == 0), stop=(k == KC - 1))
                q.then_inc(s.unit.h, 1)

        @block.scalar
        def _(act):
            evacuate(act, 0)

        @block.vector
        def _(dve):
            evacuate(dve, 1)


def even_prepare(nc, m, out):
    s = Names()
    (s.ld, s.sq, s.rs, s.nrm, s.kvo, s.qt, s.qte, s.wt, s.conv, s.cmz, s.dts, s.dta, s.ca, s.cv, s.cp) = fresh(nc, m, "ld sq rs nrm kvo qt qte wt conv cmz dts dta ca cv cp", "er")
    bcast = lambda ap, n: ap.to_broadcast([P, n])
    with nc.Block() as block:
        @block.sync
        def _(sp):
            loads = [(m.cos[:, :, :], m.c_cos), (m.sin[:, :, :], m.c_sin), (m.mask[:, :], m.c_mask), (m.tri[:, :, :], m.c_tri),
                     (m.bqk[:, 0, :], bcast(m.e_q_norm, HD)), (m.bqk[:, 1, :], bcast(m.e_k_norm, HD)),
                     (m.bsink[:, :], bcast(m.e_sink, QH)), (m.bskip[:, :], bcast(m.e_d_skip, SH)),
                     (m.balog[:, :], bcast(m.e_a_log.rearrange("j a h -> j (a h)"), 16)),
                     (m.bdtb[:, :], bcast(m.e_dt_bias.rearrange("j a h -> j (a h)"), 16)),
                     (m.wrow[0:CONV, :], m.e_conv_w[0]), (m.wrow[CONV:CONV + 1, :], m.e_conv_b),
                     (m.ckv[:, 0, :], m.cache_k[0, 0].rearrange("t h d -> t (h d)")),
                     (m.ckv[:, 1, :], m.cache_v[0, 0].rearrange("t h d -> t (h d)"))]
            for dst, src in loads:
                sp.dma_start(dst, src).then_inc(s.ld.h, 16)
            s.n_ld = 16 * len(loads)
            sp.dma_start(out["new_cache_v"][0, 0].rearrange("t h d -> t (h d)"), m.qkv[:, 0, 640:768]).then_inc(s.kvo.h, 16)
            sp.wait_ge(s.nrm.h, 1)
            sp.dma_start(out["new_cache_k"][0, 0].rearrange("t h d -> t (h d)"), m.qkv[:, 0, 512:640]).then_inc(s.kvo.h, 16)
            sp.wait_ge(s.kvo.h, 32)

        @block.scalar
        def _(act):
            ch = Chain(act, s.ca)
            for t in range(TILES):
                if t >= 2:
                    act.wait_ge(s.rs.h, 2 * (t - 1) - 1)
                nc.scalar.activation(m.t1[:, t % 2, :], m.qkv[:, t, 0:640], ACT.Square).then_inc(s.sq.h, 1)
                act.wait_ge(s.rs.h, 2 * t + 1)
                ch(nc.scalar.activation(m.r10s[:, t, :], m.r10[:, t, :], ACT.Ln, scale=1.0 / HD, bias=m.eps[:, 0:1]))
                nc.scalar.activation(m.r10[:, t, :], m.r10s[:, t, :], ACT.Exp, scale=-0.5).then_inc(s.rs.h, 1)
            act.wait_ge(s.ld.h, s.n_ld)
            nc.scalar.activation(m.balog[:, :], m.balog[:, :], ACT.Exp).then_inc(s.dta.h, 1)
            for t in range(TILES):
                act.wait_ge(s.qt.h, t + 1)
                for hf in range(2):
                    o = m.qTz[hf * 64:(hf + 1) * 64, :, t * P:(t + 1) * P].rearrange("p (i e) t -> p i e t", e=2)[:, :, hf, :]
                    nc.scalar.activation(o, m.ps[t % 2][hf * 64:(hf + 1) * 64, :].rearrange("p (i t) -> p i t", i=4), ACT.Copy)
                nc.scalar.activation(m.kTd[:, :, t * P:(t + 1) * P], m.ps[2 + t % 2][:, 0:256].rearrange("p (i t) -> p i t", i=2), ACT.Copy).then_inc(s.qte.h, 1)
            act.wait_ge(s.qt.h, TILES + 1)
            nc.scalar.activation(m.kTd[:, :, TOK:], m.ps[4][:, 0:256].rearrange("p (i t) -> p i t", i=2), ACT.Copy)
            act.wait_ge(s.dts.h, 1)
            ch(nc.scalar.activation(m.c48[:, :, 0:16], m.dt[:, :, :], ACT.Abs))
            ch(nc.scalar.activation(m.c48[:, :, 0:16], m.c48[:, :, 0:16], ACT.Exp, scale=-1.0))
            nc.scalar.activation(m.c48[:, :, 0:16], m.c48[:, :, 0:16], ACT.Ln, bias=1.0).then_inc(s.dta.h, 1)
            for c in range(XC):
                act.wait_ge(s.conv.h, c + 1)
                nc.scalar.activation(m.xc[:, c, :], m.xc[:, c, :], ACT.Silu, bias=m.cwb[:, c, CONV:CONV + 1]).then_inc(s.cmz.h, 1)
            nc.scalar.activation(m.z[:, :, :], m.z[:, :, :], ACT.Silu)
            act.wait_ge(s.cmz.h, XC)
            for g in range(2):
                nc.scalar.activation(m.cmz[g * 64:(g + 1) * 64, g, :], m.xc[g * 64:(g + 1) * 64, 5, :], ACT.Copy)
            nc.scalar.preload_act_table_set(EXP_LN)

        @block.gpsimd
        def _(pool):
            nc.gpsimd.memset(m.cmz[64:128, 0, :], 0.0)
            nc.gpsimd.memset(m.cmz[0:64, 1, :], 0.0)

        @block.vector
        def _(dve):
            ch = Chain(dve, s.cv)
            dve.wait_ge(s.ld.h, s.n_ld)
            dup = lambda o: o.rearrange("p (a r d) -> p a r d", a=2, r=2)
            for r in range(2):
                q = nc.vector.tensor_copy(dup(m.kdc[:, :])[:, :, r, :], m.ckv[:, 0, :].rearrange("p (a d) -> p a d", a=2))
            q.then_inc(s.cp.h, 1)
            for t in range(TILES):
                dve.wait_ge(s.sq.h, t + 1)
                nc.vector.tensor_reduce(m.r10[:, t, :], m.t1[:, t % 2, :].rearrange("p (h d) -> p h d", d=HD), AX.X, ALU.add).then_inc(s.rs.h, 1)
                dve.wait_ge(s.rs.h, 2 * t + 2)
                qk = m.qkv[:, t, 0:640].rearrange("p (h d) -> p h d", d=HD)
                ch(nc.vector.tensor_tensor(qk, qk, m.r10[:, t, :].unsqueeze(2).to_broadcast([P, 10, HD]), ALU.mult))
                nc.vector.tensor_tensor(qk[:, 0:8, :], qk[:, 0:8, :], m.bqk[:, 0:1, :].to_broadcast([P, 8, HD]), ALU.mult)
                q = nc.vector.tensor_tensor(qk[:, 8:10, :], qk[:, 8:10, :], m.bqk[:, 1:2, :].to_broadcast([P, 2, HD]), ALU.mult)
                if t == 0:
                    q.then_inc(s.nrm.h, 1)
                    dve.wait_ge(s.nrm.h, 1)
                else:
                    ch(q)
                    a, b = m.t2[:, 0, :], m.t3[:, 0, :]
                    v4 = lambda o: o.rearrange("p (h e d) -> p h e d", e=2, d=16)
                    cos = m.cos[:, t - 1, :].rearrange("p (x e d) -> p x e d", e=2, d=16)
                    sin = m.sin[:, t - 1, :].rearrange("p (x e d) -> p x e d", e=2, d=16)
                    nc.vector.tensor_tensor(a.rearrange("p (h d) -> p h d", d=HD), qk, m.cos[:, t - 1, :].unsqueeze(1).to_broadcast([P, 10, HD]), ALU.mult)
                    hx = lambda o: o.rearrange("p (h x e d) -> p h x e d", x=2, e=2, d=16)
                    for x in range(2):
                        for e in range(2):
                            q = nc.vector.tensor_tensor(hx(b)[:, :, x, e, :], hx(m.qkv[:, t, 0:640])[:, :, x, 1 - e, :],
                                                        sin[:, x, e, :].unsqueeze(1).to_broadcast([P, 10, 16]), ALU.mult)
                    ch(q)
                    ch(nc.vector.tensor_tensor(m.qkv[:, t, 0:640], a, b, ALU.add))
                if t >= 2:
                    dve.wait_ge(s.qt.h, t - 1)
                for r in range(2):
                    q = nc.vector.tensor_copy(dup(m.kd[:, t % 2, :])[:, :, r, :], qk[:, 8:10, :])
                q.then_inc(s.cp.h, 1)
            nc.vector.tensor_tensor(m.dt[:, :, :], m.dt[:, :, :], m.bdtb[:, :].unsqueeze(1).to_broadcast([P, TILES, 16]), ALU.add).then_inc(s.dts.h, 1)
            dve.wait_ge(s.wt.h, 1)
            ch(nc.vector.tensor_copy(m.cwb[:, :, :], m.ps[5][:, 0:XC * (CONV + 1)].rearrange("p (c j) -> p c j", c=XC)))
            for c in range(XC):
                ch(nc.vector.tensor_scalar(m.xc[:, c, :], m.xpad[:, c, 0:SPAN], m.cwb[:, c, 0:1], None, ALU.mult))
                for j in range(1, CONV):
                    q = nc.vector.scalar_tensor_tensor(out=m.xc[:, c, :], in0=m.xpad[:, c, j:j + SPAN], scalar=m.cwb[:, c, j:j + 1],
                                                       in1=m.xc[:, c, :], op0=ALU.mult, op1=ALU.add)
                    if j < CONV - 1:
                        ch(q)
                q.then_inc(s.conv.h, 1)
            dve.wait_ge(s.dta.h, 2)
            ch(nc.vector.tensor_scalar(m.dt[:, :, :], m.dt[:, :, :], 0.0, None, ALU.max))
            ch(nc.vector.tensor_tensor(m.dt[:, :, :], m.dt[:, :, :], m.c48[:, :, 0:16], ALU.add))
            ch(nc.vector.tensor_tensor(m.la[:, :, :], m.dt[:, :, :], m.balog[:, :].unsqueeze(1).to_broadcast([P, TILES, 16]), ALU.mult))
            ch(nc.vector.tensor_scalar(m.la[:, :, :], m.la[:, :, :], -1.0, None, ALU.mult))

        @block.tensor
        def _(pe):
            pe.wait_ge(s.ld.h, s.n_ld)
            for c in range(XC):
                q = nc.tensor.transpose(m.ps[5][:, c * (CONV + 1):(c + 1) * (CONV + 1)], m.wrow[:, c * P:(c + 1) * P], m.ident[0:CONV + 1, 0:CONV + 1])
            q.then_inc(s.wt.h, 1)
            for t in range(TILES):
                pe.wait_ge(s.cp.h, t + 2)
                if t >= 2:
                    pe.wait_ge(s.qte.h, t - 1)
                for i in range(4):
                    nc.tensor.transpose(m.ps[t % 2][:, i * P:(i + 1) * P], m.qkv[:, t, i * P:(i + 1) * P], m.ident[:, :])
                for i in range(2):
                    q = nc.tensor.transpose(m.ps[2 + t % 2][:, i * P:(i + 1) * P], m.kd[:, t % 2, i * P:(i + 1) * P], m.ident[:, :])
                q.then_inc(s.qt.h, 1)
            for i in range(2):
                q = nc.tensor.transpose(m.ps[4][:, i * P:(i + 1) * P], m.kdc[:, i * P:(i + 1) * P], m.ident[:, :])
            q.then_inc(s.qt.h, 1)


def ssd_intra(nc, m):
    s = Names()
    (s.xt, s.cb, s.seg, s.sege, s.mm, s.y, s.bc, s.e48, s.cv) = fresh(nc, m, "xt cb seg sege mm y bc e48 cv", "si")
    with nc.Block() as block:
        @block.tensor
        def _(pe):
            for t in range(TILES):
                o = off(t)
                if t >= 1:
                    pe.wait_ge(s.bc.h, t)
                for c in range(4):
                    nc.tensor.transpose(m.ps[7][:, c * P:(c + 1) * P], m.xc[:, c, o:o + P], m.ident[:, :])
                nc.tensor.transpose(m.ps[0][:, 0:P], m.xc[:, 4, o:o + P], m.ident[:, :])
                for g in range(2):
                    q = nc.tensor.matmul(m.ps[0][:, (1 + g) * P:(2 + g) * P], m.xc[:, 4, o:o + P], m.cmz[:, g, o:o + P], start=True, stop=True)
                for d in range(2):
                    la = m.la[:, t, d * 8:d * 8 + 8]
                    nc.tensor.matmul(m.ps[1][:, d * 8:d * 8 + 8], m.tri[:, d, :], la, start=True, stop=True)
                    nc.tensor.matmul(m.ps[1][:, 16 + d * 8:24 + d * 8], m.tri[:, 2 + d, :], la, start=True, stop=True)
                    q = nc.tensor.matmul(m.ps[1][:, 32 + d * 8:40 + d * 8], m.ones[:, :], la, start=True, stop=True)
                q.then_inc(s.xt.h, 1)
                for d in range(2):
                    for h in range(SH):
                        q = nc.tensor.matmul(m.ps[2 + 2 * d + h // 4][:, (h % 4) * P:(h % 4 + 1) * P],
                                             m.la[:, t, d * 8 + h:d * 8 + h + 1].to_broadcast([P, P]), m.tri[:, d, :], start=True, stop=True)
                q.then_inc(s.cb.h, 1)
                pe.wait_ge(s.mm.h, t + 1)
                for h in range(SH):
                    for d in range(2):
                        q = nc.tensor.matmul(m.ps[6][:, h * HD:(h + 1) * HD], m.seg[:, d, h, :], m.xs[:, t, h * HD:(h + 1) * HD], start=(d == 0), stop=(d == 1))
                q.then_inc(s.y.h, 1)

        @block.scalar
        def _(act):
            for t in range(TILES):
                act.wait_ge(s.xt.h, t + 1)
                nc.scalar.activation(m.xs[:, t, :], m.ps[7][:, :], ACT.Copy)
                nc.scalar.activation(m.bmt[:, t, :], m.ps[0][:, 0:P], ACT.Copy)
                nc.scalar.activation(m.c48[:, t, :], m.ps[1][:, 0:48], ACT.Copy)
                nc.scalar.activation(m.e48[:, t, :], m.ps[1][:, 0:48], ACT.Exp).then_inc(s.e48.h, 1)
                act.wait_ge(s.seg.h, t + 1)
                nc.scalar.activation(m.seg[:, :, :, :], m.seg[:, :, :, :], ACT.Exp).then_inc(s.sege.h, 1)

        @block.vector
        def _(dve):
            ch = Chain(dve, s.cv)
            for t in range(TILES):
                dve.wait_ge(s.xt.h, t + 1)
                dve.wait_ge(s.e48.h, t + 1)
                if t >= 1:
                    dve.wait_ge(s.y.h, t)
                nc.vector.tensor_tensor(m.wt48[:, t, :], m.e48[:, t, 16:32], m.dt[:, t, :], ALU.mult)
                for d in range(2):
                    nc.vector.tensor_tensor(m.cbm[:, d, :, :], m.ps[0][:, P:3 * P].rearrange("p (g t) -> p g t", g=2),
                                            m.tri[:, d:d + 1, :].to_broadcast([P, 2, P]), ALU.mult)
                dve.wait_ge(s.cb.h, t + 1)
                for d in range(2):
                    for h in range(SH):
                        q = nc.vector.tensor_scalar(m.seg[:, d, h, :], m.ps[2 + 2 * d + h // 4][:, (h % 4) * P:(h % 4 + 1) * P],
                                                    m.c48[:, t, d * 8 + h:d * 8 + h + 1], 0.0, ALU.subtract, ALU.min)
                q.then_inc(s.seg.h, 1)
                dve.wait_ge(s.sege.h, t + 1)
                for d in range(2):
                    for h in range(SH):
                        q = nc.vector.scalar_tensor_tensor(out=m.seg[:, d, h, :], in0=m.seg[:, d, h, :], scalar=m.dt[:, t, d * 8 + h:d * 8 + h + 1],
                                                           in1=m.cbm[:, d, h // 4, :], op0=ALU.mult, op1=ALU.mult)
                q.then_inc(s.mm.h, 1)
                dve.wait_ge(s.y.h, t + 1)
                nc.vector.tensor_copy(m.y[:, t, :], m.ps[6][:, :]).then_inc(s.bc.h, 1)


def ssd_scan(nc, m, out):
    s = Names()
    (s.ld, s.so, s.xw, s.up, s.st, s.sto, s.ca, s.cv, s.sq, s.rs) = fresh(nc, m, "ld so xw up st sto ca cv sq rs", "ss")
    steps = [(0, 0), (0, 1)]
    for n in range(4):
        steps += [(1 + n, 0), (4 - n, 1)]
    with nc.Block() as block:
        @block.sync
        def _(sp):
            for d in range(2):
                for g in range(2):
                    sp.dma_start(m.st[g * 64:(g + 1) * 64, d, :, :], m.state_ssd[0, 0, d, 4 * g:4 * g + 4].rearrange("h n p -> n h p")).then_inc(s.ld.h, 16)
            sp.dma_start(m.bnorm[:, :], m.e_ssd_norm.to_broadcast([P, DI])).then_inc(s.ld.h, 16)
            sp.wait_ge(s.st.h, 2)
            for d in range(2):
                for g in range(2):
                    sp.dma_start(out["new_state_ssd"][0, 0, d, 4 * g:4 * g + 4].rearrange("h n p -> n h p"), m.stc[g * 64:(g + 1) * 64, d, :, :]).then_inc(s.so.h, 16)
            sp.wait_ge(s.so.h, 64)

        @block.tensor
        def _(pe):
            for n, (t, d) in enumerate(steps):
                o = off(t)
                b = n % 2
                if n >= 2:
                    pe.wait_ge(s.st.h, n - 1)
                    if n == 2:
                        pe.wait_ge(s.ld.h, 80)
                    for g in range(2):
                        q = nc.tensor.matmul(m.ps[b][:, g * 256:(g + 1) * 256], m.cmz[:, g, o:o + P], m.st[:, d, :, :].rearrange("p h d -> p (h d)"), start=True, stop=True)
                    q.then_inc(s.sto.h, 1)
                pe.wait_ge(s.xw.h, n + 1)
                nc.tensor.matmul(m.ps[2 + b][:, :], m.bmt[:, t, :], m.xw[:, b, :], start=True, stop=True).then_inc(s.up.h, 1)

        @block.vector
        def _(dve):
            ch = Chain(dve, s.cv)
            hd = lambda o: o.rearrange("p (h d) -> p h d", d=HD)
            dve.wait_ge(s.ld.h, 80)
            for n, (t, d) in enumerate(steps):
                b = n % 2
                if n >= 2:
                    dve.wait_ge(s.up.h, n - 1)
                nc.vector.tensor_tensor(hd(m.xw[:, b, :]), hd(m.xs[:, t, :]), m.wt48[:, t, d * 8:d * 8 + 8].unsqueeze(2).to_broadcast([P, SH, HD]), ALU.mult).then_inc(s.xw.h, 1)
                if n >= 2:
                    dve.wait_ge(s.sto.h, n - 1)
                    ch(nc.vector.tensor_tensor(hd(m.yt[:, b, :]), hd(m.ps[b][:, :]), m.e48[:, t, d * 8:d * 8 + 8].unsqueeze(2).to_broadcast([P, SH, HD]), ALU.mult))
                    ch(nc.vector.tensor_tensor(m.y[:, t, :], m.y[:, t, :], m.yt[:, b, :], ALU.add))
                dve.wait_ge(s.up.h, n + 1)
                for g in range(2):
                    r = slice(g * 64, (g + 1) * 64)
                    new = m.ps[2 + b][r, g * 256:(g + 1) * 256].rearrange("p (h d) -> p h d", h=4)
                    if n < 2:
                        q = nc.vector.tensor_copy(m.stc[r, d, :, :], new)
                    else:
                        ch(nc.vector.tensor_tensor(m.st[r, d, :, :], m.st[r, d, :, :], m.e48[r, t, 32 + d * 8 + 4 * g:36 + d * 8 + 4 * g].unsqueeze(2).to_broadcast([64, 4, HD]), ALU.mult))
                        q = nc.vector.tensor_tensor(m.st[r, d, :, :], m.st[r, d, :, :], new, ALU.add)
                q.then_inc(s.st.h, 1)
                dve.wait_ge(s.st.h, n + 1)
            for t in range(TILES):
                ch(nc.vector.tensor_tensor(hd(m.yt[:, 0, :]), hd(m.xs[:, t, :]), m.bskip[:, :].unsqueeze(2).to_broadcast([P, SH, HD]), ALU.mult))
                ch(nc.vector.tensor_tensor(m.y[:, t, :], m.y[:, t, :], m.yt[:, 0, :], ALU.add))
                nc.vector.tensor_tensor(m.y[:, t, :], m.y[:, t, :], m.z[:, t, :], ALU.mult).then_inc(s.sq.h, 1)
                dve.wait_ge(s.rs.h, t + 1)
                nc.vector.scalar_tensor_tensor(out=m.y[:, t, :], in0=m.y[:, t, :], scalar=m.rs[:, t:t + 1], in1=m.bnorm[:, :], op0=ALU.mult, op1=ALU.mult)

        @block.scalar
        def _(act):
            ch = Chain(act, s.ca)
            for t in range(TILES):
                act.wait_ge(s.sq.h, t + 1)
                ch(nc.scalar.activation(m.pjunk[:, :], m.y[:, t, :], ACT.Square, accum_out=m.ss[:, t:t + 1]))
                ch(nc.scalar.activation(m.ss[:, t:t + 1], m.ss[:, t:t + 1], ACT.Ln, scale=1.0 / DI, bias=m.eps[:, 0:1]))
                nc.scalar.activation(m.rs[:, t:t + 1], m.ss[:, t:t + 1], ACT.Exp, scale=-0.5).then_inc(s.rs.h, 1)


def attention(nc, m):
    s = Names()
    (s.sc, s.sd, s.mxs, s.pe, s.pt, s.pte, s.o, s.od, s.ca, s.cv) = fresh(nc, m, "sc sd mxs pe pt pte o od ca cv", "at")
    units = [(t, h) for t in range(TILES) for h in range(QH)]

    def blocks(t):
        if t == 0:
            return [(1, 0)]
        r = [(1, t), (2, TILES)]
        if t > 1:
            r = [(0, t - 1)] + r
        if t < TILES - 1:
            r = r + [(3, t + 1)]
        return r

    def cols(t):
        b = [x for x, _ in blocks(t)]
        return min(b) * P, (max(b) + 1) * P

    with nc.Block() as block:
        @block.tensor
        def _(pe):
            def scores(n):
                t, h = units[n]
                if n >= 2:
                    pe.wait_ge(s.sd.h, n - 1)
                for b, kt in blocks(t):
                    q = nc.tensor.matmul(m.ps[n % 2][:, b * P:(b + 1) * P], m.qTz[:, h, t * P:(t + 1) * P], m.kTd[:, h // 4, kt * P:(kt + 1) * P], start=True, stop=True)
                q.then_inc(s.sc.h, 1)

            def values(n):
                t, h = units[n]
                pe.wait_ge(s.pe.h, n + 1)
                if n >= 2:
                    pe.wait_ge(s.pte.h, n - 1)
                for b, _ in blocks(t):
                    q = nc.tensor.transpose(m.ps[2 + n % 2][:, b * P:(b + 1) * P], m.pr[:, n % 2, b * P:(b + 1) * P], m.ident[:, :])
                q.then_inc(s.pt.h, 1)
                pe.wait_ge(s.pte.h, n + 1)
                if h == 0 and t >= 2:
                    pe.wait_ge(s.od.h, t - 1)
                bl = blocks(t)
                for k, (b, kt) in enumerate(bl):
                    v = m.ckv[:, 1, (h // 4) * HD:(h // 4 + 1) * HD] if kt == TILES else m.qkv[:, kt, 640 + (h // 4) * HD:640 + (h // 4 + 1) * HD]
                    q = nc.tensor.matmul(m.ps[4 + t % 2][:, h * HD:(h + 1) * HD], m.pT[:, n % 2, b * P:(b + 1) * P], v, start=(k == 0), stop=(k == len(bl) - 1))
                q.then_inc(s.o.h, 1)

            for n in range(len(units)):
                scores(n)
                if n >= 1:
                    values(n - 1)
            values(len(units) - 1)

        @block.vector
        def _(dve):
            ch = Chain(dve, s.cv)

            for n, (t, h) in enumerate(units):
                lo, hi = cols(t)
                dve.wait_ge(s.sc.h, n + 1)
                if n >= 2:
                    dve.wait_ge(s.pt.h, n - 1)
                q = nc.vector.scalar_tensor_tensor(out=m.pr[:, n % 2, lo:hi], in0=m.ps[n % 2][:, lo:hi], scalar=HD ** -0.5, in1=m.mask[:, lo:hi], op0=ALU.mult, op1=ALU.add)
                q.then_inc(s.sd.h, 1)
                dve.wait_ge(s.sd.h, n + 1)
                ch(nc.vector.tensor_reduce(m.mx[:, t, h:h + 1], m.pr[:, n % 2, lo:hi], AX.X, ALU.max))
                nc.vector.tensor_scalar(m.mx[:, t, h:h + 1], m.mx[:, t, h:h + 1], m.bsink[:, h:h + 1], -1.0, ALU.max, ALU.mult).then_inc(s.mxs.h, 1)

        @block.scalar
        def _(act):
            ch = Chain(act, s.ca)
            for n, (t, h) in enumerate(units):
                lo, hi = cols(t)
                act.wait_ge(s.mxs.h, n + 1)
                nc.scalar.activation(m.pr[:, n % 2, lo:hi], m.pr[:, n % 2, lo:hi], ACT.Exp, bias=m.mx[:, t, h:h + 1], accum_out=m.smx[:, t, h:h + 1]).then_inc(s.pe.h, 1)
                nc.scalar.activation(m.sk[:, t, h:h + 1], m.bsink[:, h:h + 1], ACT.Exp, bias=m.mx[:, t, h:h + 1])
                act.wait_ge(s.pt.h, n + 1)
                nc.scalar.activation(m.pT[:, n % 2, lo:hi], m.ps[2 + n % 2][:, lo:hi], ACT.Copy).then_inc(s.pte.h, 1)
                if h == QH - 1:
                    act.wait_ge(s.o.h, QH * (t + 1))
                    nc.scalar.activation(m.oa[:, t, :], m.ps[4 + t % 2][:, :], ACT.Copy).then_inc(s.od.h, 1)
    with nc.Block() as block:
        @block.vector
        def _(dve):
            ch = Chain(dve, s.cv)
            ch.n = QH * TILES
            ch(nc.vector.tensor_tensor(m.sk[:, :, :], m.sk[:, :, :], m.smx[:, :, :], ALU.add))
            ch(nc.vector.reciprocal(m.sk[:, :, :], m.sk[:, :, :]))
            nc.vector.tensor_tensor(m.oa[:, :, :].rearrange("p t (h d) -> p (t h) d", d=HD), m.oa[:, :, :].rearrange("p t (h d) -> p (t h) d", d=HD),
                                    m.sk[:, :, :].rearrange("p t h -> p (t h)").unsqueeze(2).to_broadcast([P, TILES * QH, HD]), ALU.mult)


def out_project(nc, m, w_out, rows, tag):
    s = Names()
    (s.w0, s.w1, s.tp, s.tpe, s.mm, s.ev, s.cv) = fresh(nc, m, "w0 w1 tp tpe mm ev cv", tag)
    sw = (s.w0, s.w1)
    units = [(b, t) for b in range(2) for t in range(TILES)]
    w = w_out.rearrange("(k p) n -> p k n", p=P)
    with nc.Block() as block:
        @block.sync
        def _(sp):
            for b in range(2):
                sp.dma_start(m.ew[:, b, :, :], w[:, :, b * 512:(b + 1) * 512]).then_inc(sw[b].h, 16)
            sp.wait_ge(s.w1.h, 16)

        @block.tensor
        def _(pe):
            if rows:
                for t in range(TILES):
                    if t >= 1:
                        pe.wait_ge(s.tpe.h, t)
                    for c in range(KC):
                        q = nc.tensor.transpose(m.ps[c // 4][:, (c % 4) * P:(c % 4 + 1) * P], rows(t, c), m.ident[:, :])
                    q.then_inc(s.tp.h, 1)
                pe.wait_ge(s.tpe.h, TILES)
            for n, (b, t) in enumerate(units):
                if t == 0:
                    pe.wait_ge(sw[b].h, 16)
                if n >= 4:
                    pe.wait_ge(s.ev.h, n - 3)
                for k in range(KC):
                    q = nc.tensor.matmul(m.ps[4 + n % 4][:, :], m.mixT[:, k, t * P:(t + 1) * P], m.ew[:, b, k, :], start=(k == 0), stop=(k == KC - 1))
                q.then_inc(s.mm.h, 1)

        @block.scalar
        def _(act):
            if rows:
                for t in range(TILES):
                    act.wait_ge(s.tp.h, t + 1)
                    for b in range(2):
                        q = nc.scalar.activation(m.mixT[:, 4 * b:4 * b + 4, t * P:(t + 1) * P], m.ps[b][:, :].rearrange("p (c t) -> p c t", c=4), ACT.Copy)
                    q.then_inc(s.tpe.h, 1)

        @block.vector
        def _(dve):
            for n, (b, t) in enumerate(units):
                dve.wait_ge(s.mm.h, n + 1)
                o = m.oproj[:, n % 2, :]
                nc.vector.tensor_tensor(o, m.ps[4 + n % 4][:, :], m.gate[:, cond_of(t), b * 512:(b + 1) * 512], ALU.mult).then_inc(s.ev.h, 1)
                dve.wait_ge(s.ev.h, n + 1)
                xv = m.x[:, t, b * 512:(b + 1) * 512]
                nc.vector.tensor_tensor(xv, xv, o, ALU.add)


def even_layer(nc, m, out):
    even_project(nc, m)
    even_prepare(nc, m, out)
    ssd_intra(nc, m)
    ssd_scan(nc, m, out)
    attention(nc, m)
    out_project(nc, m, m.e_w_out[0], lambda t, c: m.oa[:, t, c * P:(c + 1) * P] if c < 4 else m.y[:, t, (c - 4) * P:(c - 3) * P], "eo")


HH = 8
LEV = 7


def odd_memory(nc, m, Arena, sb):
    r = Arena()
    m.OT = r.take(KC, TOK)
    m.qg = r.take(2, TILES, 2 * P)
    m.av = r.take(2, TILES, P)
    m.alf = r.take(2, TILES, 2 * P)
    m.osb = r.take(TILES, P)
    m.So = r.take(TILES, P)
    m.kt = r.take(2, 2, P)
    m.gn = r.take(P)
    m.kq = r.take(2, 3, P)
    m.kv0 = r.take(2, 2, P)
    m.dec = r.take(TILES, 2)
    m.otri = r.take(4, P)
    assert r.at <= 15360, r.at
    r = Arena(20480)
    m.ow = r.take(2, KC, 5, P)
    m.akk = r.take(2, TILES, 2 * P)
    m.raw, m.lsg = r.take(2, 512), r.take(2, 512)
    m.cumS = r.take(3 * 129)
    m.E = r.take(2, 2, LEV, P)
    m.qE = r.take(TILES, 2, P)
    m.ex = r.take(2, 2, P)
    m.kvs = r.take(4, 2, P)
    m.ST = r.take(2, 8, P)
    m.lmask = sb("lmask", [P, LEV, P], mybir.dt.uint8)


def strided(ap, offset, dims):
    return bass.AP(ap.tensor, ap.offset + offset, [list(ap.ap[0])] + [list(d) for d in dims])


def odd_scan(nc, m, out):
    s = Names()
    (s.ld, s.st0, s.st1, s.w0, s.w1, s.so0, s.so1, s.pj, s.pje, s.ln, s.ak, s.ae, s.a2, s.p0, s.EK, s.T, s.c1, s.D,
     s.E, s.c2, s.mu, s.S, s.kvc, s.pr, s.stt, s.o, s.f1, s.f2, s.ott, s.ot, s.ca, s.cv) = fresh(nc, m, "ld st0 st1 w0 w1 so0 so1 pj pje ln ak ae a2 p0 EK T c1 D E c2 mu S kvc pr stt o f1 f2 ott ot ca cv", "oh")
    s.w, s.so, s.st = (s.w0, s.w1), (s.so0, s.so1), (s.st0, s.st1)
    w_in = m.o_w_in[0].rearrange("(k p) n -> p k n", p=P)
    groups = (0, 4 * D, D, 2 * D, 3 * D)
    ps = m.ps

    def ebuf(b, t):
        return (b + t) % 2

    def heads(eng, body):
        body(0, 0, 0, True, False)
        with eng.Fori(0, HH // 2 - 1) as i:
            body(2 * i + 1, i, 1, False, False)
            body(2 * i + 2, i + 1, 0, False, False)
        body(HH - 1, HH // 2 - 1, 1, False, True)

    def load(sp, n, b):
        for j, g in enumerate(groups):
            sp.dma_start(m.ow[:, b, :, j, :], w_in[:, :, bass.ds(n * P + g, P)]).then_inc(s.w[b].h, 16)

    def first_weights(sp):
        load(sp, 0, 0)
        load(sp, 1, 1)

    norm_phase(nc, m, 1, 0, first_weights)
    with nc.Block() as block:
        @block.sync
        def _(sp):
            def state(ap, d, n):
                return ap[0, 0].rearrange("d h k v -> k (d h) v")[:, bass.ds(n + d * HH, 1), :].rearrange("k o v -> k (o v)")

            def load_states(n, b):
                sp.dma_start(m.ST[:, b, 0, :], state(m.state_hgrn, 0, n)).then_inc(s.st[b].h, 16)
                sp.dma_start(m.ST[:, b, 7, :], state(m.state_hgrn, 1, n)).then_inc(s.st[b].h, 16)

            def store_states(n, b):
                sp.wait_ge(s.kvc.h, 5 * n + 2)
                for d in range(2):
                    sp.dma_start(state(out["new_state_hgrn"], d, n), m.kv0[:, b, d, :]).then_inc(s.so[b].h, 16)

            sp.dma_start(m.E[:, 0, 0, :, :], m.c_lmask).then_inc(s.ld.h, 16)
            sp.dma_start(m.otri[:, :, :], m.c_tri).then_inc(s.ld.h, 16)
            sp.dma_start(m.gn[:, 0:64], m.o_g_norm[:, 0:64].to_broadcast([P, 64])).then_inc(s.so0.h, 16)
            sp.dma_start(m.gn[:, 64:128], m.o_g_norm[:, 64:128].to_broadcast([P, 64])).then_inc(s.so1.h, 16)
            load_states(0, 0)
            load_states(1, 1)
            with sp.Fori(0, HH // 2 - 1) as i:
                for b in range(2):
                    n = 2 * i + b
                    sp.wait_ge(s.pj.h, 5 * n + 5)
                    load(sp, n + 2, b)
                    store_states(n, b)
                    sp.wait_ge(s.o.h, n + 1)
                    load_states(n + 2, b)
            store_states(HH - 2, 0)
            store_states(HH - 1, 1)
            for b in range(2):
                sp.wait_ge(s.w[b].h, 80 * HH // 2)
                sp.wait_ge(s.so[b].h, 16 + 32 * HH // 2)
                sp.wait_ge(s.st[b].h, 32 * HH // 2)

        @block.gpsimd
        def _(pool):
            def stage_a(n, b, t):
                x = ebuf(b, t)
                pool.wait_ge(s.ln.h, 5 * n + (t + 1))
                pool.nop(nofuse=True)
                nc.gpsimd.tensor_scalar(m.alf[:, b, t, :], m.raw[:, x, 256:512], 0.0, None, ALU.min)
                nc.gpsimd.tensor_scalar(m.qg[:, b, t, :], m.raw[:, x, 0:256], 0.0, None, ALU.min).then_inc(s.p0.h, 1)
                pool.wait_ge(s.p0.h, 10 * n + (2 * t + 1))
                nc.gpsimd.tensor_tensor(m.alf[:, b, t, :], m.alf[:, b, t, :], m.lsg[:, x, 256:512], ALU.subtract)
                nc.gpsimd.tensor_tensor(m.lsg[:, x, 0:256], m.qg[:, b, t, :], m.lsg[:, x, 0:256], ALU.subtract).then_inc(s.p0.h, 1)
                pool.wait_ge(s.p0.h, 10 * n + (2 * t + 2))
                nc.gpsimd.tensor_tensor(m.akk[:, b, t, :], m.alf[:, b, t, :], m.raw[:, x, 256:512], ALU.subtract).then_inc(s.ak.h, 1)
                pool.wait_ge(s.ae.h, 5 * n + (t + 1))
                nc.gpsimd.tensor_tensor(m.qg[:, b, t, :], m.raw[:, x, 0:256], m.lsg[:, x, 0:256], ALU.mult).then_inc(s.a2.h, 1)

            nc.gpsimd.memset(m.dec[:, 4, :], 0.0).then_inc(s.a2.h, 2)
            for t in range(TILES):
                stage_a(0, 0, t)
            with pool.Fori(0, HH // 2 - 1) as i:
                for b in (1, 0):
                    for t in range(TILES):
                        stage_a(2 * i + (2 - b), b, t)
            for t in range(TILES):
                stage_a(HH - 1, 1, t)

        @block.tensor
        def _(pe):
            def proj(n, half, b, t):
                pe.wait_ge(s.w[b].h, 80 * half + 80)
                pe.wait_ge(s.pje.h, 5 * n + (t + 1))
                for k in range(KC):
                    nc.tensor.matmul(ps[0][:, :], m.hT[:, k, t * P:(t + 1) * P], m.ow[:, b, k, 0:4, :].rearrange("p g n -> p (g n)"), start=(k == 0), stop=(k == KC - 1))
                for k in range(KC):
                    q = nc.tensor.matmul(ps[1][:, 0:P], m.hT[:, k, t * P:(t + 1) * P], m.ow[:, b, k, 4, :], start=(k == 0), stop=(k == KC - 1))
                q.then_inc(s.pj.h, 1)

            for t in range(TILES):
                proj(0, 0, 0, t)

            def prepare(n, b, t):
                pe.wait_ge(s.a2.h, 5 * n + (t + 3))
                pe.wait_ge(s.mu.h, 5 * n + (t + 1))
                pe.wait_ge(s.kvc.h, 5 * n + (t + 1))
                nc.tensor.transpose(ps[2][:, 0:P], m.qg[:, b, t, 0:P], m.ident[:, :])
                for d in range(2):
                    nc.tensor.transpose(ps[2][:, (1 + d) * P:(2 + d) * P], m.akk[:, b, t, d * P:(d + 1) * P], m.ident[:, :])
                for j, d in enumerate((0, 1, 0)):
                    nc.tensor.matmul(ps[3][:, j * P:(j + 1) * P], m.alf[:, b, t, d * P:(d + 1) * P], m.otri[:, d, :], start=True, stop=True)
                for d in range(2):
                    q = nc.tensor.matmul(ps[4][:, d * P:(d + 1) * P], m.otri[:, 2 + d, :], m.alf[:, b, t, d * P:(d + 1) * P], start=True, stop=True)
                q.then_inc(s.T.h, 1)

            def turn_outputs(n):
                pe.wait_ge(s.f2.h, n + 1)
                for t in range(TILES):
                    o = ps[7][:, t * P:(t + 1) * P] if t < 4 else ps[6][:, 0:P]
                    q = nc.tensor.transpose(o, m.osb[:, t, :], m.ident[:, :])
                q.then_inc(s.ott.h, 1)

            def head(n, half, b, first, last):
                for t in range(TILES):
                    if t > 0:
                        prepare(n, b, t)
                    if not last:
                        if b == 0:
                            proj(n + 1, half, 1, t)
                        else:
                            proj(n + 1, half + 1, 0, t)
                    if t == 0 and not first:
                        turn_outputs(n - 1)
                    pe.wait_ge(s.mu.h, 5 * n + (t + 2))
                    pe.wait_ge(s.c2.h, 5 * n + (t + 1))
                    pe.wait_ge(s.pr.h, 5 * n + (t + 1))
                    if t == 0:
                        pe.wait_ge(s.ot.h, n + 1)
                    x = ebuf(b, t)
                    for d in range(2):
                        nc.tensor.matmul(ps[5][:, 0:P], m.kq[:, x, 1 + d, :], m.kq[:, x, 0, :], start=(d == 0), stop=(d == 1))
                    for l in range(LEV):
                        r = l + 1
                        nc.tensor.matmul(ps[5 + r // 4][:, (r % 4) * P:(r % 4 + 1) * P], m.E[:, x, 0, l, :], m.E[:, x, 1, l, :], start=True, stop=True)
                    for d in range(2):
                        q = nc.tensor.matmul(ps[4][:, (2 + d) * P:(3 + d) * P], m.kt[:, x, d, :], m.av[:, b, t, :], start=True, stop=True)
                    q.then_inc(s.S.h, 1)
                if not last:
                    prepare(n + 1, 1 - b, 0)
                pe.wait_ge(s.stt.h, n + 1)
                pe.wait_ge(s.ot.h, n + 1)
                for t in range(TILES):
                    o = ps[7][:, t * P:(t + 1) * P] if t < 4 else ps[6][:, 0:P]
                    q = nc.tensor.matmul(o, m.So[:, t, :], m.av[:, b, t, :], start=True, stop=(t == 0))
                    if t > 0:
                        nc.tensor.matmul(o, m.qE[:, t, 0, :], m.ST[:, b, t - 1, :], start=False, stop=False)
                        q = nc.tensor.matmul(o, m.qE[:, t, 1, :], m.ST[:, b, 4 + t - 1, :], start=False, stop=True)
                q.then_inc(s.o.h, 1)
            pe.wait_ge(s.ld.h, 32)
            prepare(0, 0, 0)
            heads(pe, head)
            turn_outputs(HH - 1)

        @block.scalar
        def _(act):
            ch = Chain(act, s.ca)

            def stage_a(n, b, t):
                x = ebuf(b, t)
                act.wait_ge(s.pj.h, 5 * n + (t + 1))
                act.wait_ge(s.a2.h, 5 * n + (t + 1))
                nc.scalar.activation(m.av[:, b, t, :], ps[1][:, 0:P], ACT.Copy)
                nc.scalar.activation(m.raw[:, x, :], ps[0][:, :], ACT.Copy).then_inc(s.pje.h, 1)
                act.wait_ge(s.pje.h, 5 * n + (t + 2))
                ch(nc.scalar.activation(m.lsg[:, x, :], m.raw[:, x, :], ACT.Abs))
                ch(nc.scalar.activation(m.lsg[:, x, :], m.lsg[:, x, :], ACT.Exp, scale=-1.0))
                nc.scalar.activation(m.lsg[:, x, :], m.lsg[:, x, :], ACT.Ln, bias=1.0).then_inc(s.ln.h, 1)

            def stage_e(n, b, t):
                x = ebuf(b, t)
                act.wait_ge(s.ak.h, 5 * n + (t + 1))
                nc.scalar.activation(m.akk[:, b, t, :], m.akk[:, b, t, :], ACT.Exp)
                nc.scalar.activation(m.lsg[:, x, 0:256], m.lsg[:, x, 0:256], ACT.Exp).then_inc(s.ae.h, 1)

            nc.scalar.activation(m.dec[:, 0, :], m.eps[:, 0:1].to_broadcast([P, 2]), ACT.Copy).then_inc(s.pje.h, 1)
            nc.scalar.activation(m.dec[:, 1, :], m.eps[:, 0:1].to_broadcast([P, 2]), ACT.Copy).then_inc(s.ot.h, 1)
            nc.scalar.activation(m.dec[:, 2, :], m.eps[:, 0:1].to_broadcast([P, 2]), ACT.Copy).then_inc(s.kvc.h, 1)
            for t in range(TILES):
                stage_a(0, 0, t)
                stage_e(0, 0, t)

            def keep_outputs(n):
                act.wait_ge(s.ott.h, n + 1)
                act.nop(nofuse=True)
                nc.scalar.activation(m.OT[:, bass.ds(n, 1), 0:512].rearrange("p a t -> p (a t)"), ps[7][:, :], ACT.Copy)
                nc.scalar.activation(m.OT[:, bass.ds(n, 1), 512:TOK].rearrange("p a t -> p (a t)"), ps[6][:, 0:P], ACT.Copy).then_inc(s.ot.h, 1)

            def head(n, half, b, first, last):
                for t in range(TILES):
                    x = ebuf(b, t)
                    act.wait_ge(s.T.h, 5 * n + (t + 1))
                    nc.scalar.activation(m.cumS[:, 1:129], ps[3][:, 0:P], ACT.Copy)
                    nc.scalar.activation(m.cumS[:, 129:257], ps[3][:, P:2 * P], ACT.Copy)
                    nc.scalar.activation(m.cumS[:, 259:387], ps[3][:, 0:P], ACT.Copy).then_inc(s.c1.h, 1)
                    nc.scalar.activation(m.kq[:, x, :, :].rearrange("p a b -> p (a b)"), ps[2][:, 0:3 * P], ACT.Copy)
                    nc.scalar.activation(m.ex[:, 0, :, :].rearrange("p a b -> p (a b)"), ps[4][:, 0:2 * P], ACT.Exp)
                    act.wait_ge(s.D.h, 10 * n + (2 * t + 1))
                    nc.scalar.activation(m.E[:, x, 0, :, :], m.E[:, x, 0, :, :], ACT.Exp, scale=-1.0).then_inc(s.EK.h, 1)
                    act.wait_ge(s.D.h, 10 * n + (2 * t + 2))
                    nc.scalar.activation(m.E[:, x, 1, :, :], m.E[:, x, 1, :, :], ACT.Exp).then_inc(s.E.h, 1)
                    nc.scalar.activation(m.dec[:, t, 0:1], ps[3][:, P - 1:P], ACT.Exp)
                    nc.scalar.activation(m.dec[:, t, 1:2], ps[3][:, P:P + 1], ACT.Exp)
                    nc.scalar.activation(m.ex[:, 1, :, :].rearrange("p a b -> p (a b)"), ps[3][:, 0:2 * P], ACT.Exp).then_inc(s.c2.h, 1)
                    if t == 0 and not first:
                        keep_outputs(n - 1)
                    if not last:
                        stage_a(n + 1, 1 - b, t)
                    act.wait_ge(s.S.h, 5 * n + (t + 1))
                    if t == 0:
                        act.wait_ge(s.so[b].h, 32 * half + 16)
                        kv = m.kv0[:, b, :, :]
                    else:
                        kv = m.kvs[:, t - 1, :, :]
                    nc.scalar.activation(kv.rearrange("p a b -> p (a b)"), ps[4][:, 2 * P:4 * P], ACT.Copy).then_inc(s.kvc.h, 1)
                    if not last:
                        stage_e(n + 1, 1 - b, t)
                act.wait_ge(s.o.h, n + 1)
                nc.scalar.activation(m.osb[:, 0:4, :].rearrange("p t v -> p (t v)"), ps[7][:, :], ACT.Copy, scale=P ** -0.5)
                ch(nc.scalar.activation(m.osb[:, 4, :], ps[6][:, 0:P], ACT.Copy, scale=P ** -0.5))
                for t in range(TILES):
                    q = nc.scalar.activation(m.So[:, t, :], m.osb[:, t, :], ACT.Square, accum_out=m.ss[:, t:t + 1])
                ch(q)
                ch(nc.scalar.activation(m.ss[:, :], m.ss[:, :], ACT.Ln, scale=1.0 / P, bias=m.eps[:, 0:1]))
                nc.scalar.activation(m.rs[:, :], m.ss[:, :], ACT.Exp, scale=-0.5).then_inc(s.f1.h, 1)

            run_chained(ch, act, head, heads, 2 * TILES, 3)
            keep_outputs(HH - 1)

        @block.vector
        def _(dve):
            ch = Chain(dve, s.cv)

            def pred(n, t):
                dve.wait_ge(s.S.h, 5 * n + (t + 1))
                ch(nc.vector.tensor_tensor(m.So[:, t, :], ps[5][:, 0:P], m.ident[:, :], ALU.mult))
                for l in range(LEV):
                    r = l + 1
                    if l == 0:
                        dve.nop(nofuse=True)
                    q = nc.vector.copy_predicated(m.So[:, t, :], m.lmask[:, l, :], ps[5 + r // 4][:, (r % 4) * P:(r % 4 + 1) * P])
                    if l < LEV - 1:
                        ch(q)
                        dve.nop(nofuse=True)
                q.then_inc(s.pr.h, 1)

            for j, q in enumerate((s.mu, s.pr)):
                nc.vector.memset(m.ss[:, j:j + 1], 1.0).then_inc(q.h, 1)
            dve.wait_ge(s.ld.h, 32)
            ch(nc.vector.tensor_copy(m.lmask[:, :, :], m.E[:, 0, 0, :, :]))
            dve.wait_ge(s.so0.h, 16)
            dve.wait_ge(s.so1.h, 16)

            def head(n, half, b, first, last):
                for t in range(TILES):
                    x = ebuf(b, t)
                    if t > 0:
                        pred(n, t - 1)
                    dve.wait_ge(s.c1.h, 5 * n + (t + 1))
                    dve.nop(nofuse=True)
                    for side in range(2):
                        for l in range(LEV):
                            hs = 1 << l
                            nb = P // (2 * hs)
                            out_v = strided(m.E[:, x, side, l, :], 0, [(2 * hs, nb), (hs, 2), (1, hs)])
                            in_v = strided(ps[3], side * P, [(2 * hs, nb), (P + hs, 2), (1, hs)])
                            ref = strided(m.cumS, side * 129 + hs, [(2 * hs, nb), (129, 2), (0, hs)])
                            q = nc.vector.tensor_tensor(out_v, in_v, ref, ALU.subtract)
                        q.then_inc(s.D.h, 1)
                    dve.wait_ge(s.EK.h, 5 * n + (t + 1))
                    for l in range(LEV):
                        hs = 1 << l
                        nb = P // (2 * hs)
                        v = strided(m.E[:, x, 0, l, :], 0, [(2 * hs, nb), (hs, 2), (1, hs)])
                        nc.vector.tensor_tensor(v, strided(ps[2], P, [(2 * hs, nb), (P + hs, 2), (1, hs)]), v, ALU.mult)
                    dve.wait_ge(s.E.h, 5 * n + (t + 1))
                    nc.vector.tensor_tensor(m.E[:, x, 1, :, :], ps[2][:, 0:P].unsqueeze(1).to_broadcast([P, LEV, P]), m.E[:, x, 1, :, :], ALU.mult)
                    dve.wait_ge(s.c2.h, 5 * n + (t + 1))
                    nc.vector.tensor_tensor(m.kt[:, x, :, :].rearrange("p a b -> p (a b)"), m.akk[:, b, t, :], m.ex[:, 0, :, :].rearrange("p a b -> p (a b)"), ALU.mult)
                    nc.vector.tensor_tensor(m.qE[:, t, :, :], ps[2][:, 0:P].unsqueeze(1).to_broadcast([P, 2, P]), m.ex[:, 1, :, :], ALU.mult).then_inc(s.mu.h, 1)
                pred(n, TILES - 1)
                dve.wait_ge(s.kvc.h, 5 * n + 6)
                dve.wait_ge(s.st[b].h, 32 * half + 32)
                for j in range(3):
                    for d, t in ((0, 1 + j), (1, 4 - j)):
                        src = t - 1 + 4 * d
                        dst = src + 1 if d == 0 else src - 1
                        q = nc.vector.scalar_tensor_tensor(out=m.ST[:, b, dst, :], in0=m.ST[:, b, src, :], scalar=m.dec[:, t, d:d + 1], in1=m.kvs[:, t - 1, d, :], op0=ALU.mult, op1=ALU.add)
                    if j < 2:
                        ch(q)
                q.then_inc(s.stt.h, 1)
                dve.wait_ge(s.f1.h, n + 1)
                ch(nc.vector.tensor_tensor(m.osb[:, :, :], m.osb[:, :, :], m.rs[:, :].unsqueeze(2).to_broadcast([P, TILES, P]), ALU.mult))
                ch(nc.vector.tensor_tensor(m.osb[:, :, :], m.osb[:, :, :], m.gn[:, :].unsqueeze(1).to_broadcast([P, TILES, P]), ALU.mult))
                nc.vector.tensor_tensor(m.osb[:, :, :], m.osb[:, :, :], m.qg[:, b, :, P:2 * P], ALU.mult).then_inc(s.f2.h, 1)

            run_chained(ch, dve, head, heads, 0, TILES * LEV + 4)


def run_chained(ch, eng, head, heads, a_steps, b_steps):
    base = ch.n
    per = a_steps + b_steps

    def body(n, half, b, first, last):
        ch.n = n * per + base
        k0 = ch.k
        head(n, half, b, first, last)
        assert ch.k - k0 == (b_steps if last else per), (ch.k - k0, per)
    heads(eng, body)


def odd_layer(nc, m, out):
    odd_scan(nc, m, out)
    m.mixT = m.OT
    out_project(nc, m, m.o_w_out[0], None, "oo")


def constants():
    i = np.arange(P)
    t = {"ident": np.eye(P, dtype=np.float32)}
    t["iota"] = np.broadcast_to(np.arange(TOPK, dtype=np.float32), (P, TOPK)).copy()
    tri = [i[:, None] <= i[None], i[:, None] >= i[None], i[:, None] > i[None], i[:, None] < i[None]]
    t["tri"] = np.stack([x.astype(np.float32) for x in tri], 1)
    t["ones"] = np.ones((P, P), np.float32)
    lv = [((i[:, None] >> (l + 1)) == (i[None] >> (l + 1))) & ((i[:, None] >> l) != (i[None] >> l)) for l in range(LEV)]
    t["lmask"] = np.stack([x.astype(np.float32) for x in lv], 1)
    far = np.float32(-1e30)
    z = np.zeros((P, P), np.float32)
    t["mask"] = np.concatenate([np.where(i[None] >= i[:, None], z, far), z, z, np.where(i[None] <= i[:, None], z, far)], 1)
    pos = np.arange(LAT)
    inv = np.float32(10000.0) ** (-np.arange(0, 32, 2, dtype=np.float32) / np.float32(32))
    ang = np.stack([(pos // 64).astype(np.float32)[:, None] * inv, (pos % 64).astype(np.float32)[:, None] * inv], 1)
    cos, sin = np.cos(ang).astype(np.float32), np.sin(ang).astype(np.float32)
    t["cos"] = np.stack([cos, cos], 2).reshape(4, P, 64).transpose(1, 0, 2).copy()
    t["sin"] = np.stack([-sin, sin], 2).reshape(4, P, 64).transpose(1, 0, 2).copy()
    t["eps"] = np.full((P, 1), EPS, np.float32)
    return t


def build(nc, a, out):
    m = Names()
    m.x_prompt = a["x_prompt"]
    m.x_sample = a["x_sample"]
    m.cache_k = a["cache_k"]
    m.cache_v = a["cache_v"]
    m.state_ssd = a["state_ssd"]
    m.state_hgrn = a["state_hgrn"]
    m.c = a["c"]
    m.c_ctx = a["c_ctx"]
    m.w_ada = a["w_ada"]
    m.b_ada = a["b_ada"]
    m.norm_mix = a["norm_mix"]
    m.norm_ffn = a["norm_ffn"]
    m.e_w_in = a["e_w_in"]
    m.e_q_norm = a["e_q_norm"]
    m.e_k_norm = a["e_k_norm"]
    m.e_sink = a["e_sink"]
    m.e_conv_w = a["e_conv_w"]
    m.e_conv_b = a["e_conv_b"]
    m.e_dt_bias = a["e_dt_bias"]
    m.e_a_log = a["e_a_log"]
    m.e_d_skip = a["e_d_skip"]
    m.e_ssd_norm = a["e_ssd_norm"]
    m.e_w_out = a["e_w_out"]
    m.o_w_in = a["o_w_in"]
    m.o_lb = a["o_lb"]
    m.o_g_norm = a["o_g_norm"]
    m.o_w_out = a["o_w_out"]
    m.p_w_q = a["p_w_q"]
    m.p_sub_keys = a["p_sub_keys"]
    m.p_u = a["p_u"]
    m.p_v = a["p_v"]
    m.c_ident = a["c_ident"]
    m.c_iota = a["c_iota"]
    m.c_tri = a["c_tri"]
    m.c_ones = a["c_ones"]
    m.c_lmask = a["c_lmask"]
    m.c_mask = a["c_mask"]
    m.c_cos = a["c_cos"]
    m.c_sin = a["c_sin"]
    m.c_eps = a["c_eps"]
    ctx = m.ctx = ExitStack()
    with ctx:
        def sb(name, shape, dt=F32):
            return ctx.enter_context(nc.sbuf_tensor(name, shape, dt))

        psall = ctx.enter_context(nc.psum_tensor("psall", [P, 8 * 512], F32))
        m.ps = [psall[:, 512 * b:512 * (b + 1)] for b in range(8)]
        m.mod = nc.dram_tensor("mod_rows", [12 * DEPTH, D], F32, kind="Internal").ap()

        s = m.sems = Names()
        (s.bc, s.ca, s.cv, s.rs, s.tp, s.tpfree, s.hr, s.keys, s.kt, s.ktc, s.qp, s.qc, s.spd, s.sc, s.ist,
         s.ufree, s.vfree, s.ix, s.smx, s.sme, s.wr, s.dg, s.acc, s.accfree, s.cond, s.condm, s.condt,
         s.condr, s.ce, s.const, s.mp, s.mc, s.mrow, s.modst, s.outd) = fresh(nc, m, "bc ca cv rs tp tpfree hr keys kt ktc qp qc spd sc ist ufree vfree ix smx sme wr dg acc accfree "
                           "cond condm condt condr ce const mp mc mrow modst outd", "t")
        s.wq = [Sem(ctx.enter_context(nc.semaphore(f"s_wq{b}"))) for b in range(4)]
        s.ud = [Sem(ctx.enter_context(nc.semaphore(f"s_u{b}"))) for b in range(RING)]
        s.vd = [Sem(ctx.enter_context(nc.semaphore(f"s_v{b}"))) for b in range(RING)]

        m.x = sb("x", [P, TILES, D])
        m.gate = sb("gate", [P, 2, D])
        m.ident = sb("ident", [P, P])
        m.iota = sb("iota", [P, TOPK])
        m.eps = sb("eps", [P, 1])
        m.zeros = sb("zeros", [P, 512])
        m.ss = sb("ss", [P, TILES])
        m.rs = sb("rs", [P, TILES])
        WORK = 44200
        work = sb("work", [P, WORK])

        class Arena:

            def __init__(self, at=0):
                self.at = at

            def take(self, *dims):
                n = int(np.prod(dims))
                v = work[:, self.at:self.at + n]
                self.at += n
                assert self.at <= WORK, self.at
                if len(dims) > 1:
                    names = "abcd"[:len(dims)]
                    v = v.rearrange("p (" + " ".join(names) + ") -> p " + " ".join(names), **dict(zip(names, dims)))
                return v

        r = Arena()
        m.wa = r.take(4, KC, 512)
        m.mrow = r.take(DEPTH, 6 * D)
        m.brow = r.take(DEPTH, 6 * D)
        m.condr = r.take(P)[0:16, :]
        m.ce = r.take(16)
        m.condT = r.take(KC, 2)
        m.nrow = [m.gate, r.take(2, D)]
        m.ones = sb("ones", [P, P])
        m.const_loads = [(m.iota[:, :], m.c_iota), (m.eps[:, :], m.c_eps), (m.ones[:, :], m.c_ones)]
        r = Arena()
        m.h = r.take(TILES, D)
        m.S = r.take(TILES, 2 * PH * P)
        m.bc = m.S[:, 0:2, :].rearrange("p c (k d) -> p c k d", k=2)
        front = r.at
        m.hT = r.take(KC, TOK)
        m.wq = r.take(2, KC, 256)
        m.keys = r.take(2 * PH, P)
        m.keysT = r.take(2 * PH * P)
        m.qT = r.take(2, TOK)
        r2 = Arena(front)
        m.ur = r2.take(RING, D)
        m.vr = r2.take(RING, D)
        r = Arena(max(r.at, r2.at))
        m.dgb = r.take(DIAGS, P)
        m.cs, m.cs2 = r.take(256), r.take(256)
        m.tv, m.tif, m.bv = r.take(2, TOPK), r.take(2, TOPK), r.take(TOPK)
        m.pf, m.oh, m.ek, m.ef = r.take(2, TOPK), r.take(2 * TOPK, TOPK), r.take(2 * TOPK), r.take(TOPK)
        m.d16, m.dots, m.gx, m.sm, m.sr = r.take(TOPK), r.take(P), r.take(P), r.take(P), r.take(PH)
        m.bs, m.wt = r.take(2, P), r.take(2, P)
        m.junk = r.take(D)
        m.ti, m.bp, m.pi = sb("ti", [P, 2, TOPK], U32), sb("bp", [P, TOPK], U32), sb("pi", [P, 2, TOPK], U32)
        m.idx, m.iu, m.iv = sb("idx", [P, 3, P], U32), sb("iu", [P, TOPK], U32), sb("iv", [P, TOPK], U32)
        m.acc = [psall[:, 0:D], psall[:, D:2 * D]]
        m.h2p = psall[:, 2 * D:3 * D]
        even_memory(nc, m, Arena)
        odd_memory(nc, m, Arena, sb)
        m.oproj = m.cmz[:, :, 0:512]
        m.n_const = 16 * (len(m.const_loads) + 2 + 3 * DEPTH)

        setup_phase(nc, m)
        for l in range(DEPTH):
            if l == 0:
                even_layer(nc, m, out)
            else:
                odd_layer(nc, m, out)
            router_phase(nc, m, l)
            gather_phase(nc, m, l)
        with nc.Block() as block:
            @block.sync
            def _(sp):
                sp.dma_start(out["y_prompt"][0], m.x[:, 0, :]).then_inc(s.outd.h, 16)
                sp.dma_start(out["y_sample"][0].rearrange("(t p) d -> p t d", p=P), m.x[:, 1:, :]).then_inc(s.outd.h, 16)
                sp.wait_ge(s.outd.h, s.outd.at(32))


_INS = ['x_prompt', 'x_sample', 'cache_k', 'cache_v', 'state_ssd', 'state_hgrn', 'c', 'c_ctx', 'w_ada', 'b_ada', 'norm_mix',
        'norm_ffn', 'e_w_in', 'e_q_norm', 'e_k_norm', 'e_sink', 'e_conv_w', 'e_conv_b', 'e_dt_bias', 'e_a_log', 'e_d_skip',
        'e_ssd_norm', 'e_w_out', 'o_w_in', 'o_lb', 'o_g_norm', 'o_w_out', 'p_w_q', 'p_sub_keys', 'p_u', 'p_v']
_OUTS = [("y_prompt", (1, 128, 1024)), ("y_sample", (1, 512, 1024)), ("new_cache_k", (1, 1, 128, 2, 64)),
         ("new_cache_v", (1, 1, 128, 2, 64)), ("new_state_ssd", (1, 1, 2, 8, 64, 64)), ("new_state_hgrn", (1, 1, 2, 8, 128, 128))]


def kernel(**inputs):
    import concourse.bacc as bacc
    from concourse.bass_utils import run_bass_kernel_spmd

    nc = bacc.Bacc("TRN2", target_bir_lowering=False, num_devices=1)
    arrays, args, out = {}, {}, {}
    host = {n: inputs[n] for n in _INS}
    host.update({"c_" + n: t for n, t in constants().items()})
    for name, value in host.items():
        v = np.ascontiguousarray(value)
        arrays["in_" + name] = v
        args[name] = nc.dram_tensor("in_" + name, v.shape, mybir.dt.from_np(v.dtype), kind="ExternalInput").ap()
    for name, shape in _OUTS:
        out[name] = nc.dram_tensor("out_" + name, shape, F32, kind="ExternalOutput").ap()
    build(nc, args, out)
    r = run_bass_kernel_spmd(nc, [arrays], core_ids=[0])
    return tuple(r.results[0]["out_" + name] for name, _ in _OUTS)
```
